# Optimizing a Trainium2 kernel written in Bass

```python
import jax, jax.numpy as jnp
from jax import lax
import numpy as np

D_MODEL = 1024
BATCH = 1
SEQ = 512
DEPTH = 2
DEC_BATCH = 8
DEC_SEQ = 4
PAST_LEN = 4096
PAGE_SIZE = 128

HEAD_SIZE = 64
N_HEADS = D_MODEL // HEAD_SIZE
D_RWKV = N_HEADS * HEAD_SIZE
D_CONV = D_MODEL // 2
CONV_WIDTH = 31
LORA_DECAY = 64
LORA_ICLR = 64
LORA_GATE = 128
D_FF = 2816
SHIFT_W = 3 * D_RWKV + LORA_DECAY + LORA_ICLR + LORA_GATE
IN_W = SHIFT_W + 2 * D_CONV + 2 * D_MODEL
NORM_EPS = 1e-6
GN_EPS = 64e-5
LN_EPS = 1e-5

kernel_name = "rwkv7_conformer_conv_gated_hybrid_step"

def _rmsnorm(x, g):
    xf = x.astype(jnp.float32)
    y = xf * lax.rsqrt(jnp.mean(xf * xf, axis=-1, keepdims=True) + NORM_EPS)
    return (y * g.astype(jnp.float32)).astype(x.dtype)

def _swiglu(h, wg, wu, wd):
    return (jax.nn.silu(h @ wg) * (h @ wu)) @ wd

def _wkv_scan(S0, r, w, k, v, a_vec, b_vec):
    def step(S, inp):
        r_t, w_t, k_t, v_t, a_t, b_t = inp
        sa = jnp.einsum('bhij,bhj->bhi', S, a_t)
        S = S * w_t[:, :, None, :] + sa[..., None] * b_t[:, :, None, :] + v_t[..., None] * k_t[:, :, None, :]
        y = jnp.einsum('bhij,bhj->bhi', S, r_t)
        return S, y
    seq = tuple(jnp.swapaxes(t, 0, 1) for t in (r, w, k, v, a_vec, b_vec))
    S, ys = lax.scan(step, S0, seq)
    return jnp.swapaxes(ys, 0, 1), S

def _mixer(h, shift_prev, S0, conv_buf, p):
    B, T, _ = h.shape
    y = h @ p['w_in']
    ys = y[..., :SHIFT_W]
    ys_prev_row = shift_prev @ p['w_in'][:, :SHIFT_W]
    ys_prev = jnp.concatenate([ys_prev_row[:, None, :], ys[:, :-1]], axis=1)
    xs = (ys + (ys_prev - ys) * p['mu']).astype(jnp.float32)
    o0 = D_RWKV; o1 = 2 * D_RWKV; o2 = 3 * D_RWKV
    o3 = o2 + LORA_DECAY; o4 = o3 + LORA_ICLR
    r, k, v = xs[..., :o0], xs[..., o0:o1], xs[..., o1:o2]
    xw, xa, xg = xs[..., o2:o3], xs[..., o3:o4], xs[..., o4:]
    f32 = lambda t: t.astype(jnp.float32)
    w_log = -jax.nn.softplus(-(f32(p['w0']) + jnp.tanh(xw) @ f32(p['w_decay_up']))) - 0.5
    decay = jnp.exp(-jnp.exp(w_log))
    a = jax.nn.sigmoid(f32(p['a0']) + xa @ f32(p['w_iclr_up']))
    g = jax.nn.sigmoid(xg) @ f32(p['w_gate_up'])
    hs = lambda t: t.reshape(B, T, N_HEADS, HEAD_SIZE)
    kk = hs(k * f32(p['k_k']))
    kk = kk / jnp.maximum(jnp.sqrt(jnp.sum(kk * kk, axis=-1, keepdims=True)), 1e-12)
    k = k * (1.0 + (a - 1.0) * f32(p['k_a']))
    rh, kh, vh, ah = hs(r), hs(k), hs(v), hs(a)
    out, S_new = _wkv_scan(S0.astype(jnp.float32), rh, hs(decay), kh, vh, -kk, kk * ah)
    mean = jnp.mean(out, axis=-1, keepdims=True)
    var = jnp.mean(jnp.square(out - mean), axis=-1, keepdims=True)
    gn = ((out - mean) * lax.rsqrt(var + GN_EPS)).reshape(B, T, D_RWKV)
    gn = gn * f32(p['ln_x_g']) + f32(p['ln_x_b'])
    bonus = jnp.sum(rh * kh * f32(p['r_k']), axis=-1, keepdims=True) * vh
    o_a = ((gn + bonus.reshape(B, T, D_RWKV)) * g).astype(h.dtype)
    c = y[..., SHIFT_W:SHIFT_W + 2 * D_CONV]
    u = c[..., :D_CONV] * jax.nn.sigmoid(c[..., D_CONV:])
    up = jnp.concatenate([conv_buf.astype(u.dtype), u], axis=1)
    dw = lax.conv_general_dilated(up, p['conv_w'][:, None, :], (1,), 'VALID',
                                  dimension_numbers=('NWC', 'WIO', 'NWC'),
                                  feature_group_count=D_CONV) + p['conv_b']
    new_buf = up[:, -(CONV_WIDTH - 1):]
    dwf = dw.astype(jnp.float32)
    m = jnp.mean(dwf, axis=-1, keepdims=True)
    vv = jnp.mean(jnp.square(dwf - m), axis=-1, keepdims=True)
    ln = ((dwf - m) * lax.rsqrt(vv + LN_EPS) * f32(p['conv_ln_g']) + f32(p['conv_ln_b'])).astype(h.dtype)
    o_b = jax.nn.silu(ln) @ p['w_conv_out']
    g_a = jax.nn.sigmoid(y[..., SHIFT_W + 2 * D_CONV:SHIFT_W + 2 * D_CONV + D_MODEL])
    g_b = jax.nn.sigmoid(y[..., SHIFT_W + 2 * D_CONV + D_MODEL:])
    z = g_a * o_a + g_b * o_b
    return z @ p['w_out'], h[:, -1], S_new, new_buf

def _layer(x, shift_prev, S0, conv_buf, p):
    x = x + 0.5 * _swiglu(_rmsnorm(x, p['ffn1_norm']), p['ffn1_w_gate'], p['ffn1_w_up'], p['ffn1_w_down'])
    h = _rmsnorm(x, p['mix_norm'])
    mix, new_shift, S_new, new_buf = _mixer(h, shift_prev, S0, conv_buf, p)
    x = x + mix
    x = x + 0.5 * _swiglu(_rmsnorm(x, p['ffn2_norm']), p['ffn2_w_gate'], p['ffn2_w_up'], p['ffn2_w_down'])
    return x, new_shift, S_new, new_buf

def setup_inputs(seed: int = 0) -> dict:
    key = jax.random.key(seed)
    ks = iter(jax.random.split(key, 40))
    nrm = lambda shape, s: jax.random.normal(next(ks), shape, jnp.float32) * s
    gain = lambda shape: 1.0 + nrm(shape, 0.02)
    L, D, F, DA, DC = DEPTH, D_MODEL, D_FF, D_RWKV, D_CONV
    w0_base = jnp.linspace(-6.0, -1.0, DA, dtype=jnp.float32)
    return {
        'x_prompt': nrm((BATCH, SEQ, D), 1.0),
        'x_sample': nrm((DEC_BATCH, DEC_SEQ, D), 1.0),
        'state_wkv': nrm((L, DEC_BATCH, N_HEADS, HEAD_SIZE, HEAD_SIZE), 0.3),
        'state_shift': nrm((L, DEC_BATCH, D), 1.0),
        'state_conv': nrm((L, DEC_BATCH, CONV_WIDTH - 1, DC), 0.5),
        'ffn1_norm': gain((L, D)),
        'ffn1_w_gate': nrm((L, D, F), D ** -0.5),
        'ffn1_w_up': nrm((L, D, F), D ** -0.5),
        'ffn1_w_down': nrm((L, F, D), F ** -0.5),
        'mix_norm': gain((L, D)),
        'w_in': nrm((L, D, IN_W), D ** -0.5),
        'mu': jax.random.uniform(next(ks), (L, SHIFT_W), jnp.float32),
        'w0': w0_base[None, :] + nrm((L, DA), 0.1),
        'w_decay_up': nrm((L, LORA_DECAY, DA), 0.5 * LORA_DECAY ** -0.5),
        'a0': nrm((L, DA), 0.1),
        'w_iclr_up': nrm((L, LORA_ICLR, DA), 0.5 * LORA_ICLR ** -0.5),
        'w_gate_up': nrm((L, LORA_GATE, DA), LORA_GATE ** -0.5),
        'k_k': 0.85 + nrm((L, DA), 0.02),
        'k_a': gain((L, DA)),
        'r_k': nrm((L, N_HEADS, HEAD_SIZE), 0.1),
        'ln_x_g': gain((L, DA)),
        'ln_x_b': nrm((L, DA), 0.02),
        'conv_w': nrm((L, CONV_WIDTH, DC), CONV_WIDTH ** -0.5),
        'conv_b': nrm((L, DC), 0.02),
        'conv_ln_g': gain((L, DC)),
        'conv_ln_b': nrm((L, DC), 0.02),
        'w_conv_out': nrm((L, DC, D), DC ** -0.5),
        'w_out': nrm((L, D, D), D ** -0.5),
        'ffn2_norm': gain((L, D)),
        'ffn2_w_gate': nrm((L, D, F), D ** -0.5),
        'ffn2_w_up': nrm((L, D, F), D ** -0.5),
        'ffn2_w_down': nrm((L, F, D), F ** -0.5),
        'final_norm': gain((D,)),
    }

def reference(x_prompt, x_sample, state_wkv, state_shift, state_conv,
              ffn1_norm, ffn1_w_gate, ffn1_w_up, ffn1_w_down, mix_norm, w_in, mu,
              w0, w_decay_up, a0, w_iclr_up, w_gate_up, k_k, k_a, r_k, ln_x_g, ln_x_b,
              conv_w, conv_b, conv_ln_g, conv_ln_b, w_conv_out, w_out,
              ffn2_norm, ffn2_w_gate, ffn2_w_up, ffn2_w_down, final_norm):
    xp, xs = x_prompt, x_sample
    Bp = x_prompt.shape[0]
    sp_shift = jnp.zeros((Bp, D_MODEL), x_prompt.dtype)
    sp_wkv = jnp.zeros((Bp, N_HEADS, HEAD_SIZE, HEAD_SIZE), jnp.float32)
    sp_conv = jnp.zeros((Bp, CONV_WIDTH - 1, D_CONV), x_prompt.dtype)
    wkv_p, shift_p, conv_p, wkv_s, shift_s, conv_s = [], [], [], [], [], []
    for l in range(DEPTH):
        p = {
            'ffn1_norm': ffn1_norm[l], 'ffn1_w_gate': ffn1_w_gate[l], 'ffn1_w_up': ffn1_w_up[l],
            'ffn1_w_down': ffn1_w_down[l], 'mix_norm': mix_norm[l], 'w_in': w_in[l], 'mu': mu[l],
            'w0': w0[l], 'w_decay_up': w_decay_up[l], 'a0': a0[l], 'w_iclr_up': w_iclr_up[l],
            'w_gate_up': w_gate_up[l], 'k_k': k_k[l], 'k_a': k_a[l], 'r_k': r_k[l],
            'ln_x_g': ln_x_g[l], 'ln_x_b': ln_x_b[l], 'conv_w': conv_w[l], 'conv_b': conv_b[l],
            'conv_ln_g': conv_ln_g[l], 'conv_ln_b': conv_ln_b[l], 'w_conv_out': w_conv_out[l],
            'w_out': w_out[l], 'ffn2_norm': ffn2_norm[l], 'ffn2_w_gate': ffn2_w_gate[l],
            'ffn2_w_up': ffn2_w_up[l], 'ffn2_w_down': ffn2_w_down[l],
        }
        xp, sh, S, cb = _layer(xp, sp_shift, sp_wkv, sp_conv, p)
        shift_p.append(sh); wkv_p.append(S.astype(x_prompt.dtype)); conv_p.append(cb)
        xs, sh, S, cb = _layer(xs, state_shift[l], state_wkv[l], state_conv[l], p)
        shift_s.append(sh.astype(state_shift.dtype)); wkv_s.append(S.astype(state_wkv.dtype))
        conv_s.append(cb.astype(state_conv.dtype))
    y_prompt = _rmsnorm(xp, final_norm)
    y_sample = _rmsnorm(xs, final_norm)
    return (y_prompt, y_sample, jnp.stack(wkv_p), jnp.stack(shift_p), jnp.stack(conv_p),
            jnp.stack(wkv_s), jnp.stack(shift_s), jnp.stack(conv_s))


_drawn_inputs = setup_inputs


def setup_inputs(seed=0):
    import zlib

    import numpy as np

    out = dict(_drawn_inputs(seed))
    spreads = {}
    factors = {'ffn1_norm': 3.51,
     'ln_x_g': 30.956,
     'ln_x_b': 29.409,
     'conv_b': 3.168,
     'conv_ln_g': 20.618,
     'conv_ln_b': 20.585,
     'ffn2_norm': 5.147,
     'final_norm': 7.484,
     'r_k': 2.758}
    for name, (base, spread) in spreads.items():
        noise = np.random.default_rng([zlib.crc32(name.encode()), seed]).standard_normal(out[name].shape)
        drawn = base * np.exp(spread * noise) if base else spread * noise
        out[name] = __import__('jax').numpy.asarray(drawn.astype(out[name].dtype))
    for name, factor in factors.items():
        out[name] = (out[name] * factor).astype(out[name].dtype)
    return out
```

```python
from contextlib import ExitStack

import numpy as np

import concourse.bass as bass
import concourse.mybir as mybir
from concourse.alu_op_type import AluOpType as ALU

F32 = mybir.dt.float32
ACT = mybir.ActivationFunctionType
AX = mybir.AxisListType

L = 2
D = 1024
KT = D // 128
TP = 512
NB, NT = 8, 4
TS = NB * NT
T = TP + TS
TH = T + NB
N = 64
NH = D // N
DFF = 2816
FT = DFF // 128
DC = 512
CT = DC // 128
CW = 31
HIST = CW - 1
C = 64
NC = TP // C
PAIRS = NH // 2
LEVELS = 6
KAPPA = float(np.exp(-0.5))
NORM_EPS, GN_EPS, LN_EPS = 1e-6, 64e-5, 1e-5

PARAMS = [("ffn1_norm", 8), ("mix_norm", 8), ("ffn2_norm", 8), ("mu", 26), ("w0", 8), ("a0", 8),
          ("k_k", 8), ("k_a", 8), ("r_k", 8), ("ln_x_g", 8), ("ln_x_b", 8), ("conv_b", 4),
          ("conv_ln_g", 4), ("conv_ln_b", 4), ("conv_w", CT * CW)]
COL = {}
_at = 0
for _name, _n in PARAMS:
    COL[_name] = _at
    _at += _n
NPAR = _at

Q_FFN1 = 0
Q_LORA = Q_FFN1 + FT
Q_CONV = Q_LORA + 1
Q_PAIR = Q_CONV + CT
Q_LATE = Q_PAIR + 2 * PAIRS
Q_OUT = Q_LATE + KT
Q_FFN2 = Q_OUT + KT // 2
Q_ALL = Q_FFN2 + FT
WR_ALL = Q_ALL - 2 * PAIRS - KT
K_ID, K_ONE, K_BLK, K_MASK, K_LEV, K_SCAN = 0, 128, 256, 384, 512, 512 + 384
K_EPS = K_SCAN + TP
K_ALL = K_EPS + 4


class Steps:

    def __init__(self, sem, units, names, credit=2):
        self.sem, self.units, self.names, self.credit = sem, units, list(names), credit

    def after(self, l, unit, name):
        n = len(self.names)
        return (l * self.units + unit + self.credit) * n + self.names.index(name) + 1


def build(nc, xt, par, fnorm, shf, cs, s_in, wr, wpa, wpb, wl, wd, consts,
          y_out, wkvp_out, shift_out, convp_out, wkvs_out, convs_out):
    ctx = ExitStack()
    with ctx:
        def sb(name, shape):
            return ctx.enter_context(nc.sbuf_tensor(name, shape, F32))

        def sem(name):
            return ctx.enter_context(nc.semaphore(name))

        scr_q = nc.dram_tensor("scr_q", [6 * TS, D], F32).ap()
        scr_y = nc.dram_tensor("scr_y", [NB * NH, NT * N], F32).ap()

        X = sb("X", [128, KT, T])
        H = sb("H", [128, KT, TH])
        ring_mem = [sb(f"ring{i}", [128, 2 * D + 256]) for i in range(2)]
        ring = [r[:, 0:2 * D].rearrange("p (a k m) -> p a k m", a=2, k=KT) for r in ring_mem]
        par_sb = sb("par_sb", [128, NPAR])
        fn_sb = sb("fn_sb", [128, KT])
        shf_sb = sb("shf_sb", [128, L, KT, NB])
        sho = sb("sho", [128, L, KT, 1 + NB])
        K = sb("K", [128, K_ALL])
        NR = sb("NR", [128, T])
        arena = sb("arena", [128, 36896])
        PS = ctx.enter_context(nc.psum_tensor("PS", [128, 8, 512], F32))

        ident, ones, blk = (K[:, a:a + 128] for a in (K_ID, K_ONE, K_BLK))
        mask8 = K[:, K_MASK:K_MASK + 128]
        lev = K[:, K_LEV:K_LEV + LEVELS * C].rearrange("p (l t) -> p l t", l=LEVELS)
        scan_keep = K[:, K_SCAN:K_SCAN + TP]
        eps_norm, eps_gn, eps_ln = (K[:, K_EPS + i:K_EPS + i + 1] for i in range(3))

        def P(name, i=0):
            return par_sb[:, bass.ds(COL[name] + i, 1)]

        class Take:
            def __init__(self, start):
                self.at = start

            def __call__(self, *dims):
                n = int(np.prod(dims))
                v = arena[:, self.at:self.at + n]
                self.at += n
                assert self.at <= 36896, self.at
                if len(dims) == 1:
                    return v
                names = "abcd"[:len(dims)]
                return v.rearrange(f"p ({' '.join(names)}) -> p {' '.join(names)}",
                                   **{k: d for k, d in zip(names, dims)})

        take = Take(0)
        mid = take(FT, T)
        dring = [take(FT, 128) for _ in range(2)]
        gsil = [take(T) for _ in range(2)]
        take = Take(0)
        Z = take(KT, T)
        xwa, sg = take(T), take(T)
        UP = take(CT, HIST + TP)
        US = take(CT, NB, HIST + NT)
        DW = take(CT, T)
        SQT = take(PAIRS, 6, TS)
        SX = take(PAIRS, 3, TS)
        shared = take.at
        Y3 = take(3, TH + 1)
        D3 = take(3, T)
        LW, A, CC, PP, KQ, KK, KP, T1 = (take(T) for _ in range(8))
        GT, GA, GG, BON = take(T), take(T), take(T), take(T)
        PEND = take(NC)
        BK, BKH, ZV, AR, BKT, W = (take(NC, 128) for _ in range(6))
        GM = take(2, NC, 128)
        ML = [take(2, NC, C) for _ in range(2)]
        U, XI, AS = (take(2, NC // 2, C) for _ in range(3))
        S0, XS, YO = take(128), take(128), take(TP)
        SQ = CC[:, 0:TP]
        STO = take(PAIRS, C)
        take = Take(shared)
        SS, M1, M2 = take(N, N), take(N, N), take(N, N)
        QA, QB = take(D), take(D)
        QT = take(6, NT, N)
        SA, SY, YT = take(N), take(NT, N), take(D)
        YF, YD, YR = take(PAIRS, TS), take(PAIRS, TS), take(PAIRS, TS)
        GB, OB = [take(T) for _ in range(2)], [take(T) for _ in range(2)]
        LQ = [D3[:, 0], D3[:, 1], D3[:, 2], T1]

        CG = [KK, KP]

        def slots(x):
            return x.rearrange("p (e q) (s t) -> p e (q s) t", q=2, s=2)

        def tokens(x):
            return x[:, 0:TP].rearrange("p (e q t) -> p e q t", q=2, t=C)

        def bank2(s, n):
            return PS[:, 2 * s:2 * s + 2, 0:n]

        def two(a):
            return a.rearrange("p (a b) -> p a b", a=2)

        const_load, par_load, x_load = sem("const_load"), sem("par_load"), sem("x_load")
        ring_load = [sem(f"ring_load{i}") for i in range(2)]
        d_load = [sem(f"d_load{i}") for i in range(2)]
        mix_load, s_load = sem("mix_load"), sem("s_load")
        out_done, conv_out_done = sem("out_done"), sem("conv_out_done")
        q_put, q_got, y_put, y_got, s_out = (sem(n) for n in ("q_put", "q_got", "y_put", "y_got", "s_out"))

        gemm = Steps(sem("gemm_done"), 2 * Q_ALL, ["tile"], 4)
        xdone = Steps(sem("x_updated"), 3, [f"m{m}" for m in range(KT)], 1)
        norm_a = Steps(sem("norm_act"), 3, [f"sq{k}" for k in range(KT)] + ["rt"])
        norm_p = Steps(sem("norm_pe"), 3, ["ss"])
        norm_v = Steps(sem("norm_dve"), 3, ["ri"] + [f"h{k}" for k in range(KT)])
        prev_v = Steps(sem("shift_dve"), 1, ["prev", "out0", "out1"])
        silu_a = Steps(sem("ffn_silu"), 2 * FT, ["silu"])
        mul_v = Steps(sem("ffn_mul"), 2 * FT, ["mul"])
        down_p = Steps(sem("down_pe"), 2 * KT, ["down"])
        lora_a = Steps(sem("lora_act"), 1, ["y0", "y1", "tanh", "xa", "sg"])
        lora_g = Steps(sem("lora_pool"), 1, [f"d{i}{j}" for i in range(2) for j in range(3)])
        lora_v = Steps(sem("lora_dve"), 1, ["x0", "x1"])
        glu_a = Steps(sem("glu_act"), CT, ["sig"])
        glu_v = Steps(sem("glu_dve"), CT, ["u0", "u1", "us"])
        tap_v = Steps(sem("conv_tap"), CW, [f"{s}{c}" for c in range(CT) for s in "ps"])
        cln_p = Steps(sem("conv_ln_pe"), 1, ["mean", "var"])
        cln_a = Steps(sem("conv_ln_act"), 1, [f"sq{c}" for c in range(CT)] + ["rt"] + [f"out{c}" for c in range(CT)])
        cln_v = Steps(sem("conv_ln_dve"), 1, [f"dc{c}" for c in range(CT)] + ["ri"] + [f"n{c}" for c in range(CT)])
        fp = Steps(sem("front_pe"), PAIRS, ["dec", "gate", "icl", "kk", "g0", "tb", "bon", "g1", "tz"])
        fa = Steps(sem("front_act"), PAIRS, ["y0", "y1", "lw", "y2", "sqk", "gt", "a", "rtk", "p", "ip",
                                             "pw", "zv", "ga", "tb", "tz"])
        fg = Steps(sem("front_pool"), PAIRS, [f"d{i}{j}" for i in range(3) for j in range(3)]
                   + ["s_v", "s_r", "s_kk", "s_kp", "s_b", "s_gt", "s_ga", "s_bon"])
        fv = Steps(sem("front_dve"), PAIRS, ["x0", "x1", "c", "x2", "t1", "inv0", "inv", "kk", "kp", "b", "rk",
                                             "bk_b", "bk_k", "pend", "ar_a", "ar_0", "ar_r", "hat", "bon",
                                             "g0", "g1", "gg"])
        bp = Steps(sem("back_pe"), PAIRS, ["x0"] + [f"{s}{i}" for i in range(1, LEVELS) for s in "azt"][:-1]
                   + [f"{s}_{c}" for c in range(NC) for s in ("x", "sa", "s", "y")] + ["mean", "var"])
        bg = Steps(sem("back_pool"), PAIRS, [f"ml{i}" for i in range(LEVELS)])
        bv = Steps(sem("back_dve"), PAIRS,
                   ["u0l", "u0"] + [f"{s}{i}" for i in range(1, LEVELS) for s in "ux"][:-1]
                   + [f"{s}_{c}" for c in range(NC) for s in ("sa", "sl", "sh")]
                   + ["dc", "ri", "gn", "gnb", "ob", "z"])
        ba = Steps(sem("back_act"), PAIRS, ["x0"] + [f"a{i}" for i in range(1, LEVELS)]
                   + [f"{s}_{c}" for c in range(NC) for s in ("xs", "y")] + ["sq", "rt"])
        late_a = Steps(sem("late_act"), KT, ["gb"])
        late_v = Steps(sem("late_dve"), KT, ["ob", "zp", "zs"])
        zero_g = Steps(sem("zeros_pool"), 1, ["y", "up", "zv", "s0"])
        sp_p = Steps(sem("sample_pe"), 1, ["tq0", "tq1", "ty", "mean", "var"])
        sp_a = Steps(sem("sample_act"), 1, ["qa", "qb", "yf", "sq", "rt"])
        SCAN = ["m", "sa", "u", "o", "v", "y", "r"]
        sp_v = Steps(sem("sample_dve"), NT, SCAN)
        sp_g = Steps(sem("sample_pool"), NT, ["sw", "vk"])
        spo_v = Steps(sem("sample_out"), 1, ["dc", "ri", "gn", "g", "b", "ob", "og", "oa", "z"])
        ALL_STEPS = {
            "pe": [gemm, norm_p, down_p, cln_p, fp, bp, sp_p],
            "act": [norm_a, silu_a, lora_a, glu_a, cln_a, fa, ba, late_a, sp_a],
            "dve": [xdone, norm_v, prev_v, mul_v, lora_v, glu_v, tap_v, cln_v, fv, bv, late_v, sp_v, spo_v],
            "pool": [lora_g, fg, bg, sp_g, zero_g],
        }

        waits_met = sem("waits_met")

        def grant(eng, which):
            for s in ALL_STEPS[which]:
                eng.sem_inc(s.sem, len(s.names) * s.credit)

        def alone(eng):
            eng.sem_inc(waits_met, 1)

        def tile_after(l, q, half):
            return gemm.after(l, 2 * q + half, "tile")

        RING_N = [(Q_ALL - i + 1) // 2 for i in range(2)]

        def ring_value(l, q0, j=0):
            return (l * RING_N[q0 % 2] + q0 // 2 + j + 1) * 16

        block = ctx.enter_context(nc.Block())

        @block.sync
        def _(sp):
            sp.dma_start(K[:, :], consts).then_inc(const_load, 16)
            sp.dma_start(X[:, :, :], xt).then_inc(x_load, 16)
            sp.dma_start(fn_sb[:, :], fnorm).then_inc(const_load, 16)
            sp.dma_start(shf_sb[:, :, :, :], shf).then_inc(const_load, 16)

            def load_ring(l, q0, j, src):
                q = q0 + 2 * j
                sp.wait_ge(gemm.sem, tile_after(l, q - 2, 1))
                sp.dma_start(ring_mem[q0 % 2][:, 0:src.shape[-1]], src).then_inc(ring_load[q0 % 2], 16)

            def row(w, i):
                return w[bass.ds(i, 1)].rearrange("a p n -> p (a n)")

            def wr_at(l, i):
                return row(wr, l * WR_ALL + i)

            def ffn_loads(l, f, q0, i0):
                alone(sp)
                with sp.Fori(0, FT // 2) as j:
                    for b in range(2):
                        load_ring(l, q0 + b, j, wr_at(l, i0 + b + 2 * j))
                if f == 1:
                    sp.wait_ge(xdone.sem, xdone.after(l, 1, f"m{KT - 1}"))
                alone(sp)
                with sp.Fori(0, KT // 2) as j:
                    for b in range(2):
                        sp.wait_ge(down_p.sem, down_p.after(l, f * KT + 2 * j + b - 2, "down"))
                        sp.dma_start(dring[b].rearrange("p k m -> p (k m)"),
                                     wd[bass.ds(l * 2 * KT + f * KT + 2 * j + b, 1)].rearrange("a p n -> p (a n)")
                                     ).then_inc(d_load[b], 16)

            with sp.Fori(0, L) as l:
                sp.wait_ge(xdone.sem, xdone.after(l, -1, f"m{KT - 1}"))
                sp.dma_start(par_sb[:, :], par[bass.ds(l, 1)].rearrange("a p n -> p (a n)")).then_inc(par_load, 16)
                ffn_loads(l, 0, Q_FFN1, 0)
                load_ring(l, Q_LORA, 0, wr_at(l, Q_LORA))
                sp.wait_ge(xdone.sem, xdone.after(l, 0, f"m{KT - 1}"))
                sp.dma_start(US.rearrange("p a b c -> p (a b c)"),
                             cs[bass.ds(l, 1)].rearrange("a p n -> p (a n)")).then_inc(mix_load, 16)
                with sp.Fori(0, CT // 2) as j:
                    for b in range(2):
                        load_ring(l, Q_CONV + b, j, wr_at(l, Q_CONV + b + 2 * j))
                sp.wait_ge(zero_g.sem, zero_g.after(l, 0, "zv"))
                sp.wait_ge(glu_v.sem, glu_v.after(l, CT - 1, "us"))
                sp.dma_start(convp_out[bass.ds(l, 1)].rearrange("a p c n -> p (a c) n"),
                             UP[:, :, TP:TP + HIST]).then_inc(conv_out_done, 16)
                sp.dma_start(convs_out[bass.ds(l, 1)].rearrange("a p n -> p (a n)"),
                             US.rearrange("p a b c -> p (a b c)")).then_inc(conv_out_done, 16)
                with sp.Fori(0, PAIRS) as p:
                    load_ring(l, Q_PAIR, p, row(wpa, l * PAIRS + p))
                    load_ring(l, Q_PAIR + 1, p, row(wpb, l * PAIRS + p))
                sp.wait_ge(bv.sem, bv.after(l, PAIRS - 1, "z"))
                sp.dma_start(wkvp_out[bass.ds(l, 1)].rearrange("a p n -> p (a n)"),
                             STO.rearrange("p a b -> p (a b)")).then_inc(s_out, 16)
                sp.wait_ge(fg.sem, fg.after(l, PAIRS - 1, "s_bon"))
                sp.dma_start(SS.rearrange("p a b -> p (a b)"),
                             s_in[bass.ds(l, 1)].rearrange("a p n -> p (a n)")).then_inc(s_load, 16)
                sp.wait_ge(sp_a.sem, sp_a.after(l, 0, "qa"))
                by_q = scr_q.rearrange("(b q t) n -> q b t n", b=NB, q=6)
                for i in range(6):
                    if i == 4:
                        sp.wait_ge(sp_a.sem, sp_a.after(l, 0, "qb"))
                    rows = QA[TS * i:TS * i + TS] if i < 4 else QB[TS * (i - 4):TS * (i - 4) + TS]
                    sp.dma_start(by_q[i], rows).then_inc(q_put, 16)
                sp.wait_ge(q_put, l * 96 + 96)
                for b in range(NB):
                    sp.dma_start(QT[b * NH:(b + 1) * NH].rearrange("h q t j -> h (q t) j"),
                                 scr_q.rearrange("(b q t) (h j) -> b h (q t) j", b=NB, q=6, h=NH)[b]
                                 ).then_inc(q_got, 16)
                with sp.Fori(0, KT // 2) as j:
                    for b in range(2):
                        load_ring(l, Q_LATE + b, j, wl[bass.ds(l * KT + b + 2 * j, 1)].rearrange("a p n -> p (a n)"))
                sp.wait_ge(sp_v.sem, sp_v.after(l, NT - 1, "r"))
                sp.dma_start(scr_y, SY.rearrange("p t j -> p (t j)")).then_inc(y_put, 16)
                sp.dma_start(wkvs_out[bass.ds(l, 1)].rearrange("a p n -> p (a n)"),
                             SS.rearrange("p a b -> p (a b)")).then_inc(s_out, 16)
                sp.wait_ge(y_put, l * 16 + 16)
                for b in range(NB):
                    sp.dma_start(YT[b * NT:(b + 1) * NT].rearrange("t (h j) -> t h j", h=NH),
                                 scr_y.rearrange("(b h) (t j) -> b t h j", b=NB, t=NT)[b]).then_inc(y_got, 16)
                sp.wait_ge(conv_out_done, l * 32 + 32)
                sp.wait_ge(s_out, l * 32 + 32)
                alone(sp)
                with sp.Fori(0, KT // 4) as j:
                    for b in range(2):
                        load_ring(l, Q_OUT + b, j, wr_at(l, Q_PAIR + b + 2 * j))
                ffn_loads(l, 1, Q_FFN2, Q_PAIR + KT // 2)
            sp.wait_ge(prev_v.sem, prev_v.after(L - 1, 0, "out1"))
            sp.dma_start(shift_out, sho[:, :, :, :]).then_inc(out_done, 16)
            sp.wait_ge(norm_v.sem, norm_v.after(L, 0, f"h{KT - 1}"))
            sp.dma_start(y_out, H[:, :, 0:T]).then_inc(out_done, 16)
            sp.wait_ge(out_done, 32)

        @block.gpsimd
        def _(pool):
            grant(pool, "pool")

            def diff(l, steps, unit, i, y, d):
                ys = y[:, 1 + TP:1 + T].rearrange("p (b t) -> p b t", b=NB)
                ds = d[:, TP:T].rearrange("p (b t) -> p b t", b=NB)
                pool.tensor_tensor(d[:, 0:TP], y[:, 0:TP], y[:, 1:1 + TP], ALU.subtract).then_inc(steps.sem, 1)
                pool.tensor_tensor(ds[:, :, 1:NT], ys[:, :, 0:NT - 1], ys[:, :, 1:NT], ALU.subtract
                                   ).then_inc(steps.sem, 1)
                pool.tensor_tensor(ds[:, :, 0], y[:, 1 + T:1 + TH], ys[:, :, 0], ALU.subtract
                                   ).then_inc(steps.sem, 1)

            def level(l, p, i):
                if i == 0:
                    pool.wait_ge(fv.sem, fv.after(l, p, "g1"))
                if i >= 2:
                    pool.wait_ge(bp.sem, bp.after(l, p, f"a{max(i - 2, 1)}"))
                if i == 2:
                    pool.wait_ge(bv.sem, bv.after(l, p, "u0"))
                m = lev[:, i, :].unsqueeze(1).unsqueeze(1).broadcast_to([128, 2, NC, C])
                pool.tensor_tensor(ML[i % 2], GM[:, :, :, 0:C], m, ALU.mult).then_inc(bg.sem, 1)

            def shift(l, p, i):
                pool.wait_ge(fa.sem, fa.after(l, p, f"y{i}"))
                diff(l, fg, p, i, Y3[:, i, :], D3[:, i, :])

            def keep(l, p, steps, name, dst, src):
                pool.wait_ge(steps.sem, steps.after(l, p, name))
                alone(pool)
                pool.tensor_copy(dst.rearrange("p a t -> p (a t)"), src[:, TP:T]).then_inc(fg.sem, 1)

            def keeps(l, p):
                def sqt(i):
                    return SQT[:, bass.ds(p, 1), i, :]
                keep(l, p, fv, "x2", sqt(2), D3[:, 2, :])
                keep(l, p, fv, "x0", sqt(5), D3[:, 0, :])
                keep(l, p, fv, "kk", sqt(3), KK)
                keep(l, p, fv, "kp", sqt(1), KP)
                keep(l, p, fv, "b", sqt(4), A)
                keep(l, p, fa, "gt", SX[:, bass.ds(p, 1), 1, :], GT)
                keep(l, p, fa, "ga", SX[:, bass.ds(p, 1), 2, :], GA)
                keep(l, p, fv, "bon", SX[:, bass.ds(p, 1), 0, :], BON)

            def first_pair(l):
                for i in range(3):
                    shift(l, 0, i)
                keeps(l, 0)

            def step_of_pairs(l, p):
                for i in range(4):
                    level(l, p, i)
                shift(l, p + 1, 0)
                for i in (4, 5):
                    level(l, p, i)
                for i in (1, 2):
                    shift(l, p + 1, i)
                keeps(l, p + 1)

            def scan_step(l, t):
                pool.wait_ge(sp_v.sem, sp_v.after(l, t, "m"))
                pool.tensor_tensor(SS, SS, QT[:, 0, bass.ds(t, 1), :].broadcast_to([128, N, N]), ALU.mult
                                   ).then_inc(sp_g.sem, 1)
                pool.wait_ge(sp_v.sem, sp_v.after(l, t - 1, "v"))
                pool.tensor_tensor(M2, QT[:, 2, bass.ds(t, 1), :].rearrange("p a n -> p n a").broadcast_to([128, N, N]),
                                   QT[:, 1, bass.ds(t, 1), :].broadcast_to([128, N, N]), ALU.mult
                                   ).then_inc(sp_g.sem, 1)

            with pool.Fori(0, L) as l:
                pool.wait_ge(xdone.sem, xdone.after(l, 0, f"m{KT - 1}"))
                alone(pool)
                pool.memset(Y3[:, :, 0:1], 0.0).then_inc(zero_g.sem, 1)
                pool.memset(UP[:, :, 0:HIST], 0.0).then_inc(zero_g.sem, 1)
                pool.memset(slots(ZV)[:, :, 0:4:3, :], 0.0).then_inc(zero_g.sem, 1)
                pool.memset(S0, 0.0).then_inc(zero_g.sem, 1)
                for i in range(2):
                    pool.wait_ge(lora_a.sem, lora_a.after(l, 0, f"y{i}"))
                    pool.wait_ge(zero_g.sem, zero_g.after(l, 0, "y"))
                    diff(l, lora_g, 0, i, Y3[:, i, :], D3[:, i, :])
                first_pair(l)
                with pool.Fori(0, PAIRS - 1) as p:
                    step_of_pairs(l, p)
                for i in range(LEVELS):
                    level(l, PAIRS - 1, i)
                pool.wait_ge(q_got, l * NB * 16 + NB * 16)
                alone(pool)
                with pool.Fori(0, NT) as t:
                    scan_step(l, t)

        @block.tensor
        def _(pe):
            grant(pe, "pe")

            def tile(out, w, rhs, n, kt=KT):
                for half in range(2):
                    for k in range(kt):
                        last = pe.matmul(out[:, half, :], w[:, k, :], rhs[:, k, half * n:half * n + n],
                                         start=(k == 0), stop=(k == kt - 1))
                return last

            def norm(l, i):
                pe.wait_ge(xdone.sem, xdone.after(l, i - 1, "m4"))
                for k in range(KT):
                    pe.wait_ge(norm_a.sem, norm_a.after(l, i, f"sq{k}"))
                    for half in range(2):
                        last = pe.matmul(bank2(0, T // 2)[:, half, :], ones, H[:, k, half * T // 2:half * T // 2 + T // 2],
                                         start=(k == 0), stop=(k == KT - 1), skip_group_check=True)
                last.then_inc(norm_p.sem, 1)

            def ffn(l, f, q0):
                pe.wait_ge(norm_v.sem, norm_v.after(l, 2 * f, f"h{KT - 1}"))
                alone(pe)
                with pe.Fori(0, FT // 2) as j:
                    for b in range(2):
                        pe.wait_ge(ring_load[(q0 + b) % 2], ring_value(l, q0 + b, j))
                        pe.wait_ge(silu_a.sem, silu_a.after(l, f * FT + 2 * j + b - 2, "silu"))
                        tile(bank2(2 * b, T // 2), ring[(q0 + b) % 2][:, 0], H, T // 2).then_inc(gemm.sem, 1)
                        pe.wait_ge(mul_v.sem, mul_v.after(l, f * FT + 2 * j + b - 2, "mul"))
                        tile(bank2(2 * b + 1, T // 2), ring[(q0 + b) % 2][:, 1], H, T // 2).then_inc(gemm.sem, 1)
                pe.wait_ge(mul_v.sem, mul_v.after(l, f * FT + FT - 1, "mul"))
                alone(pe)
                with pe.Fori(0, KT // 4) as j:
                    for b in range(4):
                        pe.wait_ge(d_load[b % 2], ((l * 2 + f) * (KT // 2) + 2 * j + b // 2 + 1) * 16)
                        pe.wait_ge(xdone.sem, xdone.after(l, 2 * f, "m0") + 4 * j + b - 4)
                        tile(bank2(b, T // 2), dring[b % 2], mid, T // 2, FT).then_inc(down_p.sem, 1)

            def lora(l):
                pe.wait_ge(norm_v.sem, norm_v.after(l, 1, f"h{KT - 1}"))
                pe.wait_ge(prev_v.sem, prev_v.after(l, 0, "prev"))
                pe.wait_ge(ring_load[Q_LORA % 2], ring_value(l, Q_LORA))
                for i in range(2):
                    tile(bank2(i, TH // 2), ring[Q_LORA % 2][:, i], H, TH // 2).then_inc(gemm.sem, 1)

            def conv_in(l):
                alone(pe)
                with pe.Fori(0, CT // 2) as j:
                    for b in range(2):
                        q = Q_CONV + b
                        pe.wait_ge(ring_load[q % 2], ring_value(l, q, j))
                        if b == 0:
                            pe.wait_ge(lora_a.sem, lora_a.after(l, 0, "y1"))
                        pe.wait_ge(glu_v.sem, glu_v.after(l, 2 * j + b - 2, "us"))
                        tile(bank2(2 * b, T // 2), ring[q % 2][:, 0], H, T // 2).then_inc(gemm.sem, 1)
                        pe.wait_ge(glu_a.sem, glu_a.after(l, 2 * j + b - 2, "sig"))
                        tile(bank2(2 * b + 1, T // 2), ring[q % 2][:, 1], H, T // 2).then_inc(gemm.sem, 1)

            def over_channels(l, steps, name, slot, x):
                for c in range(CT):
                    pe.wait_ge(steps.sem, steps.after(l, *name(c)))
                    for half in range(2):
                        last = pe.matmul(bank2(slot, T // 2)[:, half, :], ones, x(c)[:, half * T // 2:half * T // 2 + T // 2],
                                         start=(c == 0), stop=(c == CT - 1), skip_group_check=True)
                last.then_inc(cln_p.sem, 1)

            def conv_mean(l):
                over_channels(l, tap_v, lambda c: (CW - 1, f"s{c}"), 0, lambda c: DW[:, c, :])

            def conv_var(l):
                over_channels(l, cln_a, lambda c: (0, f"sq{c}"), 1, lambda c: LQ[c])

            def wide(out, w, rhs):
                for half in range(2):
                    last = pe.matmul(out[:, half, :], w, rhs[:, half * T // 2:half * T // 2 + T // 2],
                                     start=True, stop=True)
                return last

            F0, F1 = (bank2(i, TH // 2) for i in range(2))
            G0, G1 = (bank2(i, T // 2) for i in range(2))

            def part(l, p, i, k0, k1):
                q = Q_PAIR + i // 2
                out, n = ((F0, TH // 2), (F1, TH // 2), (F0, TH // 2), (G0, T // 2))[i]
                if k0 == 0:
                    if i % 2 == 0:
                        pe.wait_ge(ring_load[q % 2], ring_value(l, q, p))
                    if i == 0:
                        pe.wait_ge(fv.sem, fv.after(l, p - 1, "g1"))
                    elif i == 1:
                        pe.wait_ge(fa.sem, fa.after(l, p - 1, "tz"))
                    else:
                        pe.wait_ge(fa.sem, fa.after(l, p, "y0" if i == 2 else "a"))
                for k in range(k0, k1):
                    for half in range(2):
                        last = pe.matmul(out[:, half, :], ring[q % 2][:, i % 2, k, :], H[:, k, half * n:half * n + n],
                                         start=(k == 0), stop=(k == KT - 1), skip_group_check=True)
                if k1 == KT:
                    last.then_inc(gemm.sem, 1)

            def low_rank(l, p, name):
                q = (Q_PAIR + 1) % 2
                if name == "dec":
                    pe.wait_ge(ring_load[q], ring_value(l, Q_PAIR + 1, p))
                    pe.wait_ge(fa.sem, fa.after(l, p, "y1"))
                    wide(G1, ring_mem[q][0:64, 2 * D:2 * D + 128], xwa[0:64]).then_inc(fp.sem, 1)
                elif name == "gate":
                    pe.wait_ge(fa.sem, fa.after(l, p, "lw"))
                    wide(G1, ring_mem[q][:, 2 * D + 128:2 * D + 256], sg).then_inc(fp.sem, 1)
                else:
                    pe.wait_ge(fa.sem, fa.after(l, p, "y2"))
                    wide(G0, ring_mem[q][64:128, 2 * D:2 * D + 128], xwa[64:128]).then_inc(fp.sem, 1)

            def key_norm(l, p):
                pe.wait_ge(fa.sem, fa.after(l, p, "gt"))
                pe.wait_ge(fa.sem, fa.after(l, p, "sqk"))
                wide(G1, blk, KQ).then_inc(fp.sem, 1)

            def gram(l, p, h):
                base = 6 - 6 * h
                for c in range(NC):
                    r = slice(64 * h, 64 * h + 64)
                    last = pe.matmul(PS[:, base + c // 4, (c % 4) * 128:(c % 4) * 128 + 128], BK[r, c, :], AR[r, c, :],
                                     start=True, stop=True)
                last.then_inc(fp.sem, 1)

            def token_major(base, x):
                for c in range(NC):
                    last = pe.transpose(PS[:, base + c // 4, (c % 4) * 128:(c % 4) * 128 + 128], x[:, c, :], ident)
                last.then_inc(fp.sem, 1)

            def head_mean(l, p):
                pe.wait_ge(ba.sem, ba.after(l, p, f"y_{NC - 1}"))
                pe.matmul(PS[:, 4, :], blk, YO, start=True, stop=True).then_inc(bp.sem, 1)

            def head_var(l, p):
                pe.wait_ge(ba.sem, ba.after(l, p, "sq"))
                pe.matmul(PS[:, 5, :], blk, SQ, start=True, stop=True).then_inc(bp.sem, 1)

            def finish(l, p, before):
                if before is not None:
                    head_mean(l, before)
                    pe.wait_ge(bv.sem, bv.after(l, before, f"sh_{NC - 1}"))
                pe.wait_ge(fa.sem, fa.after(l, p, "rtk"))
                pe.wait_ge(fv.sem, fv.after(l, p, "ar_r"))
                gram(l, p, 0)
                pe.wait_ge(fv.sem, fv.after(l, p, "hat"))
                token_major(2, BKH)
                pe.wait_ge(fa.sem, fa.after(l, p, "ga"))
                wide(G0, blk, T1).then_inc(fp.sem, 1)
                if before is not None:
                    head_var(l, before)
                pe.wait_ge(fv.sem, fv.after(l, p, "bon"))
                gram(l, p, 1)
                pe.wait_ge(fa.sem, fa.after(l, p, "tb"))
                token_major(2, ZV)

            def first_pair(l):
                part(l, 0, 0, 0, KT)
                part(l, 0, 1, 0, KT)
                part(l, 0, 2, 0, KT)
                low_rank(l, 0, "dec")
                low_rank(l, 0, "gate")
                low_rank(l, 0, "icl")
                key_norm(l, 0)
                part(l, 0, 3, 0, KT)
                finish(l, 0, None)

            def blocks(bank, w, x):
                for h in range(2):
                    for e in range(NC // 2):
                        for q in range(2):
                            r = slice(64 * q, 64 * q + 64)
                            at = (h * (NC // 2) + e) * C
                            last = pe.matmul(PS[r, bank, at:at + C], w[r, h, e if w.shape[2] < NC else 2 * e + q, :],
                                             x[r, r] if x is ident else x[r, h, e, :], start=True, stop=True)
                return last

            def level(l, p, i, fill):
                if i == 0:
                    pe.wait_ge(bv.sem, bv.after(l, p, "u0"))
                    alone(pe)
                    blocks(4, U, ident).then_inc(bp.sem, 1)
                    return
                pe.wait_ge(bg.sem, bg.after(l, p, f"ml{i}"))
                if i == 1:
                    pe.wait_ge(ba.sem, ba.after(l, p, "x0"))
                else:
                    pe.wait_ge(bv.sem, bv.after(l, p, f"x{i - 1}"))
                alone(pe)
                blocks(5, ML[i % 2], XI).then_inc(bp.sem, 1)
                fill(0)
                pe.wait_ge(ba.sem, ba.after(l, p, f"a{i}"))
                alone(pe)
                blocks(6, AS, U).then_inc(bp.sem, 1)
                if i < LEVELS - 1:
                    blocks(7, U, AS).then_inc(bp.sem, 1)
                fill(1)

            def chunk(l, p, c, fill):
                q, e = c % 2, c // 2
                r = slice(64 * q, 64 * q + 64)
                if c == 0:
                    pe.wait_ge(bv.sem, bv.after(l, p, f"u{LEVELS - 1}"))
                    pe.wait_ge(fa.sem, fa.after(l, p, "tz"))
                if c > 0:
                    pe.wait_ge(bv.sem, bv.after(l, p, f"sh_{c - 1}"))
                    pe.matmul(PS[r, 4, 0:128], AR[:, c, 0:C], S0, start=True, stop=False, skip_group_check=True)
                for h in range(2):
                    last = pe.matmul(PS[r, 4, h * N:h * N + N], GM[:, h, c, 0:C], W[:, c, h * N:h * N + N],
                                     start=(c == 0), stop=True, skip_group_check=True)
                last.then_inc(bp.sem, 1)
                if c > 0:
                    pe.wait_ge(ba.sem, ba.after(l, p, f"y_{c - 1}"))
                    pe.matmul(PS[:, 7, 0:C], S0, AR[:, c, C:2 * C], start=True, stop=False, skip_group_check=True)
                fill(0)
                pe.wait_ge(ba.sem, ba.after(l, p, f"xs_{c}"))
                alone(pe)
                for h in range(2):
                    last = pe.matmul(PS[r, 5, h * N:h * N + N], U[r, h, e, :], XS[r, h * N:h * N + N],
                                     start=True, stop=True)
                last.then_inc(bp.sem, 1)
                fill(1)
                pe.wait_ge(bv.sem, bv.after(l, p, f"sa_{c}"))
                for h in range(2):
                    last = pe.matmul(PS[64 * h:64 * h + 64, 6, 0:N], BKT[:, c, h * N:h * N + N], W[:, c, h * N:h * N + N],
                                     start=True, stop=True)
                last.then_inc(bp.sem, 1)
                for h in range(2):
                    last = pe.matmul(PS[64 * h:64 * h + 64, 7, 0:C], W[:, c, h * N:h * N + N], GM[:, h, c, C:2 * C],
                                     start=(c == 0), stop=True, skip_group_check=True)
                last.then_inc(bp.sem, 1)
                fill(2)

            def step_of_pairs(l, p):
                n = p + 1

                def rows(i):
                    part(l, n, i // KT, i % KT, i % KT + 1)

                level(l, p, 0, None)
                rows(0)
                rows(1)
                for i in range(1, LEVELS):
                    def fill_level(s):
                        at = 3 * i - 1
                        if s == 0:
                            rows(at)
                        else:
                            rows(at + 1)
                            rows(at + 2)
                    level(l, p, i, fill_level)
                for c in range(NC):
                    def fill_chunk(s):
                        at = 3 * c + s
                        if at == 0:
                            low_rank(l, n, "dec")
                        elif at < 8:
                            rows(16 + at)
                        elif at == 8:
                            low_rank(l, n, "gate")
                        elif at == 9:
                            low_rank(l, n, "icl")
                        elif at == 11:
                            key_norm(l, n)
                        elif 12 <= at < 20:
                            part(l, n, 3, at - 12, at - 11)
                    chunk(l, p, c, fill_chunk)
                finish(l, n, p)

            def last_pair(l):
                p = PAIRS - 1
                for i in range(LEVELS):
                    level(l, p, i, lambda s: None)
                    if i == 3:
                        conv_mean(l)
                for c in range(NC):
                    chunk(l, p, c, lambda s: None)
                    if c == 1:
                        conv_var(l)
                head_mean(l, p)
                head_var(l, p)

            def late(l):
                pe.wait_ge(fg.sem, fg.after(l, PAIRS - 1, "s_bon"))
                pe.wait_ge(fv.sem, fv.after(l, PAIRS - 1, "g1"))
                for g, rows in ((0, 128), (1, 64)):
                    for p in range(PAIRS):
                        last = pe.transpose(PS[0:rows, 2 * g + p // 4, (p % 4) * 128:(p % 4) * 128 + 128],
                                            SQT[:, p, 4 * g:4 * g + rows // TS, :].rearrange("p a t -> p (a t)"), ident)
                    last.then_inc(sp_p.sem, 1)
                pe.wait_ge(cln_a.sem, cln_a.after(l, 0, f"out{CT - 1}"))
                pe.wait_ge(sp_a.sem, sp_a.after(l, 0, "qb"))
                pe.wait_ge(bv.sem, bv.after(l, PAIRS - 1, "z"))
                alone(pe)
                with pe.Fori(0, KT // 2) as j:
                    for b in range(2):
                        q = Q_LATE + b
                        pe.wait_ge(ring_load[q % 2], ring_value(l, q, j))
                        pe.wait_ge(late_a.sem, late_a.after(l, 2 * j + b - 2, "gb"))
                        tile(bank2(2 * b, T // 2), ring[q % 2][:, 0], H, T // 2).then_inc(gemm.sem, 1)
                        pe.wait_ge(late_v.sem, late_v.after(l, 2 * j + b - 2, "ob"))
                        tile(bank2(2 * b + 1, T // 2), ring[q % 2][:, 1], DW, T // 2, CT).then_inc(gemm.sem, 1)
                pe.wait_ge(y_got, l * NB * 16 + NB * 16)
                pe.wait_ge(late_a.sem, late_a.after(l, KT - 1, "gb"))
                pe.wait_ge(late_v.sem, late_v.after(l, KT - 1, "ob"))
                alone(pe)
                for p in range(PAIRS):
                    last = pe.transpose(PS[:, 0, p * TS:(p + 1) * TS], YT[0:TS, p * 128:(p + 1) * 128], ident[0:TS, 0:TS])
                last.then_inc(sp_p.sem, 1)
                pe.wait_ge(sp_a.sem, sp_a.after(l, 0, "yf"))
                pe.matmul(PS[:, 2, 0:PAIRS * TS], blk, YF.rearrange("p a t -> p (a t)"), start=True, stop=True
                          ).then_inc(sp_p.sem, 1)
                pe.wait_ge(sp_a.sem, sp_a.after(l, 0, "sq"))
                pe.matmul(PS[:, 4, 0:PAIRS * TS], blk, YR.rearrange("p a t -> p (a t)"), start=True, stop=True
                          ).then_inc(sp_p.sem, 1)

            def mix_out(l):
                pe.wait_ge(spo_v.sem, spo_v.after(l, 0, "z"))
                alone(pe)
                with pe.Fori(0, KT // 4) as j:
                    for b in range(4):
                        q = Q_OUT + b // 2
                        pe.wait_ge(ring_load[q % 2], ring_value(l, q, j))
                        pe.wait_ge(xdone.sem, xdone.after(l, 1, "m0") + 4 * j + b - 4)
                        tile(bank2(b, T // 2), ring[q % 2][:, b % 2], Z, T // 2).then_inc(gemm.sem, 1)

            pe.wait_ge(const_load, 48)
            with pe.Fori(0, L) as l:
                norm(l, 0)
                ffn(l, 0, Q_FFN1)
                norm(l, 1)
                lora(l)
                conv_in(l)
                pe.wait_ge(lora_a.sem, lora_a.after(l, 0, "sg"))
                pe.wait_ge(glu_v.sem, glu_v.after(l, CT - 1, "us"))
                pe.wait_ge(mix_load, l * 16 + 16)
                first_pair(l)
                with pe.Fori(0, PAIRS - 1) as p:
                    step_of_pairs(l, p)
                last_pair(l)
                late(l)
                mix_out(l)
                norm(l, 2)
                ffn(l, 1, Q_FFN2)
            norm(L, 0)

        @block.scalar
        def _(act):
            grant(act, "act")

            def norm(l, i):
                for k in range(KT):
                    act.wait_ge(xdone.sem, xdone.after(l, i - 1, f"m{k}"))
                    act.activation(H[:, k, 0:T], X[:, k, :], ACT.Square).then_inc(norm_a.sem, 1)
                act.wait_ge(norm_p.sem, norm_p.after(l, i, "ss"))
                act.activation(two(NR[:, :]), bank2(0, T // 2), ACT.Sqrt, scale=1.0 / D, bias=eps_norm
                               ).then_inc(norm_a.sem, 1)

            def ffn(l, f, q0):
                alone(act)
                with act.Fori(0, FT // 2) as j:
                    for b in range(2):
                        act.wait_ge(gemm.sem, tile_after(l, q0 + b + 2 * j, 0))
                        act.wait_ge(mul_v.sem, mul_v.after(l, f * FT + 2 * j + b - 2, "mul"))
                        act.activation(two(gsil[b]), bank2(2 * b, T // 2), ACT.Silu).then_inc(silu_a.sem, 1)

            def lora(l):
                for i in range(2):
                    act.wait_ge(gemm.sem, tile_after(l, Q_LORA, i))
                    act.activation(two(Y3[:, i, 1:1 + TH]), bank2(i, TH // 2), ACT.Copy).then_inc(lora_a.sem, 1)
                act.wait_ge(lora_v.sem, lora_v.after(l, 0, "x0"))
                act.activation(xwa[0:64], D3[0:64, 0, :], ACT.Tanh).then_inc(lora_a.sem, 1)
                act.activation(xwa[64:128], D3[64:128, 0, :], ACT.Copy).then_inc(lora_a.sem, 1)
                act.wait_ge(lora_v.sem, lora_v.after(l, 0, "x1"))
                act.activation(sg, D3[:, 1, :], ACT.Sigmoid).then_inc(lora_a.sem, 1)

            def glu(l):
                alone(act)
                with act.Fori(0, CT // 2) as j:
                    for b in range(2):
                        act.wait_ge(gemm.sem, tile_after(l, Q_CONV + b + 2 * j, 1))
                        act.wait_ge(glu_v.sem, glu_v.after(l, 2 * j + b - 2, "us"))
                        act.activation(two(CG[b]), bank2(2 * b + 1, T // 2), ACT.Sigmoid).then_inc(glu_a.sem, 1)

            def conv_squares(l):
                for c in range(CT):
                    if c == 0:
                        act.wait_ge(fg.sem, fg.after(l, PAIRS - 1, "s_bon"))
                    act.wait_ge(cln_v.sem, cln_v.after(l, 0, f"dc{c}"))
                    act.activation(LQ[c], DW[:, c, :], ACT.Square).then_inc(cln_a.sem, 1)

            def conv_root(l):
                act.wait_ge(cln_p.sem, cln_p.after(l, 0, "var"))
                act.activation(two(NR[:, :]), bank2(1, T // 2), ACT.Sqrt, scale=1.0 / DC, bias=eps_ln
                               ).then_inc(cln_a.sem, 1)

            def conv_silu(l):
                for c in range(CT):
                    act.wait_ge(cln_v.sem, cln_v.after(l, 0, f"n{c}"))
                    act.activation(DW[:, c, :], DW[:, c, :], ACT.Silu, scale=P("conv_ln_g", c), bias=P("conv_ln_b", c)
                                   ).then_inc(cln_a.sem, 1)

            G0, G1 = (bank2(i, T // 2) for i in range(2))

            def row_out(l, p, i):
                if i == 0:
                    act.wait_ge(fv.sem, fv.after(l, p - 1, "gg"))
                    act.wait_ge(fg.sem, fg.after(l, p - 1, "s_bon"))
                act.wait_ge(gemm.sem, tile_after(l, Q_PAIR + 2 * p + i // 2, i % 2))
                act.activation(two(Y3[:, i, 1:1 + TH]), bank2(i % 2, TH // 2), ACT.Copy).then_inc(fa.sem, 1)

            def decay(l, p):
                act.wait_ge(fp.sem, fp.after(l, p, "dec"))
                act.activation(two(LW), G1, ACT.Sigmoid, bias=P("w0", p)).then_inc(fa.sem, 1)

            def key_squares(l, p):
                act.wait_ge(fv.sem, fv.after(l, p, "x1"))
                act.activation(KQ, D3[:, 1, :], ACT.Square, scale=P("k_k", p)).then_inc(fa.sem, 1)

            def gate_rate(l, p):
                act.wait_ge(fp.sem, fp.after(l, p, "gate"))
                act.activation(two(GT), G1, ACT.Copy).then_inc(fa.sem, 1)
                act.wait_ge(fp.sem, fp.after(l, p, "icl"))
                act.activation(two(A), G0, ACT.Sigmoid, bias=P("a0", p)).then_inc(fa.sem, 1)

            def key_root(l, p):
                act.wait_ge(fp.sem, fp.after(l, p, "kk"))
                act.activation(two(KQ), G1, ACT.Sqrt).then_inc(fa.sem, 1)

            def decays(l, p):
                act.wait_ge(fv.sem, fv.after(l, p, "c"))
                act.activation(PP[:, 0:TP], CC[:, 0:TP], ACT.Exp, scale=-KAPPA).then_inc(fa.sem, 1)
                act.activation(CC[:, 0:TP], CC[:, 0:TP], ACT.Exp, scale=KAPPA).then_inc(fa.sem, 1)
                act.activation(SQT[:, bass.ds(p, 1), 0, :].rearrange("p a t -> p (a t)"), LW[:, TP:T], ACT.Exp,
                               scale=-KAPPA).then_inc(fa.sem, 1)

            def values(l, p):
                act.wait_ge(fv.sem, fv.after(l, p, "x2"))
                act.wait_ge(zero_g.sem, zero_g.after(l, 0, "s0"))
                act.activation(slots(ZV)[:, :, 1:3, :], tokens(D3[:, 2, :]), ACT.Copy).then_inc(fa.sem, 1)

            def gate_a(l, p):
                act.wait_ge(gemm.sem, tile_after(l, Q_PAIR + 2 * p + 1, 1))
                act.activation(two(GA), G0, ACT.Sigmoid).then_inc(fa.sem, 1)

            def transposed(l, p, name, dst):
                act.wait_ge(fp.sem, fp.after(l, p, name))
                act.activation(dst.rearrange("p c n -> p (c n)"), PS[:, 2:4, :].rearrange("p a b -> p (a b)"), ACT.Copy
                               ).then_inc(fa.sem, 1)

            def flat(x):
                return x.rearrange("p a b c -> p (a b c)")

            def level(l, p, i):
                if i == 0:
                    act.wait_ge(bp.sem, bp.after(l, p, "x0"))
                    act.activation(flat(XI), PS[:, 4, :], ACT.Copy).then_inc(ba.sem, 1)
                else:
                    act.wait_ge(bp.sem, bp.after(l, p, f"a{i}"))
                    act.activation(flat(AS), PS[:, 5, :], ACT.Copy).then_inc(ba.sem, 1)

            def chunk(l, p, c):
                r = slice(64 * (c % 2), 64 * (c % 2) + 64)
                act.wait_ge(bp.sem, bp.after(l, p, f"x_{c}"))
                act.activation(XS[r], PS[r, 4, 0:128], ACT.Copy).then_inc(ba.sem, 1)
                if c == 0:
                    act.wait_ge(bv.sem, bv.after(l, p - 1, "z"))
                act.wait_ge(bp.sem, bp.after(l, p, f"y_{c}"))
                act.activation(YO[:, c * C:c * C + C], PS[:, 7, 0:C], ACT.Copy).then_inc(ba.sem, 1)

            def head_squares(l, p):
                act.wait_ge(bv.sem, bv.after(l, p, "dc"))
                act.activation(SQ, YO, ACT.Square).then_inc(ba.sem, 1)

            def head_root(l, p):
                act.wait_ge(bp.sem, bp.after(l, p, "var"))
                act.activation(SQ, PS[:, 5, :], ACT.Sqrt, scale=1.0 / N, bias=eps_gn).then_inc(ba.sem, 1)

            def first_pair(l):
                row_out(l, 0, 0)
                row_out(l, 0, 1)
                decay(l, 0)
                row_out(l, 0, 2)
                key_squares(l, 0)
                gate_rate(l, 0)
                key_root(l, 0)
                decays(l, 0)
                values(l, 0)
                gate_a(l, 0)
                transposed(l, 0, "tb", BKT)
                transposed(l, 0, "tz", W)

            def step_of_pairs(l, p):
                n = p + 1
                for i in range(LEVELS):
                    level(l, p, i)
                    if i == 2:
                        row_out(l, n, 0)
                    if i == 5:
                        row_out(l, n, 1)
                for c in range(NC):
                    chunk(l, p, c)
                    if c == 0:
                        decay(l, n)
                    if c == 2:
                        row_out(l, n, 2)
                        key_squares(l, n)
                    if c == 3:
                        gate_rate(l, n)
                    if c == 4:
                        key_root(l, n)
                    if c == 5:
                        decays(l, n)
                        values(l, n)
                    if c == 6:
                        gate_a(l, n)
                head_squares(l, p)
                transposed(l, n, "tb", BKT)
                head_root(l, p)
                transposed(l, n, "tz", W)

            def last_pair(l):
                p = PAIRS - 1
                for i in range(LEVELS):
                    level(l, p, i)
                conv_squares(l)
                for c in range(NC):
                    chunk(l, p, c)
                    if c == 2:
                        conv_root(l)
                    if c == 4:
                        conv_silu(l)
                head_squares(l, p)
                head_root(l, p)

            def late(l):
                act.wait_ge(bv.sem, bv.after(l, PAIRS - 1, "z"))
                act.wait_ge(sp_p.sem, sp_p.after(l, 0, "tq0"))
                act.activation(QA, PS[:, 0:2, :].rearrange("p a b -> p (a b)"), ACT.Copy).then_inc(sp_a.sem, 1)
                act.wait_ge(sp_p.sem, sp_p.after(l, 0, "tq1"))
                act.activation(QB[0:64], PS[0:64, 2:4, :].rearrange("p a b -> p (a b)"), ACT.Copy).then_inc(sp_a.sem, 1)
                with act.Fori(0, KT // 2) as j:
                    for b in range(2):
                        act.wait_ge(gemm.sem, tile_after(l, Q_LATE + b + 2 * j, 0))
                        act.wait_ge(late_v.sem, late_v.after(l, 2 * j + b - 2, "zs"))
                        act.activation(two(GB[b]), bank2(2 * b, T // 2), ACT.Sigmoid).then_inc(late_a.sem, 1)
                act.wait_ge(sp_p.sem, sp_p.after(l, 0, "ty"))
                act.activation(YF.rearrange("p a t -> p (a t)"), PS[:, 0, 0:PAIRS * TS], ACT.Copy).then_inc(sp_a.sem, 1)
                act.wait_ge(spo_v.sem, spo_v.after(l, 0, "dc"))
                act.activation(YR.rearrange("p a t -> p (a t)"), YF.rearrange("p a t -> p (a t)"), ACT.Square
                               ).then_inc(sp_a.sem, 1)
                act.wait_ge(sp_p.sem, sp_p.after(l, 0, "var"))
                act.activation(YR.rearrange("p a t -> p (a t)"), PS[:, 4, 0:PAIRS * TS], ACT.Sqrt, scale=1.0 / N,
                               bias=eps_gn).then_inc(sp_a.sem, 1)

            act.wait_ge(const_load, 48)
            act.wait_ge(x_load, 16)
            alone(act)
            with act.Fori(0, L) as l:
                norm(l, 0)
                ffn(l, 0, Q_FFN1)
                norm(l, 1)
                lora(l)
                glu(l)
                first_pair(l)
                with act.Fori(0, PAIRS - 1) as p:
                    step_of_pairs(l, p)
                last_pair(l)
                late(l)
                norm(l, 2)
                ffn(l, 1, Q_FFN2)
            norm(L, 0)

        @block.vector
        def _(dve):
            grant(dve, "dve")
            mid2 = mid.rearrange("p t (a b) -> p (t a) b", a=2)
            X2 = X[:, :, :].rearrange("p t (a b) -> p (t a) b", a=2)

            def tt(out, a, b, op):
                return dve.tensor_tensor(out, a, b, op)

            def stt(out, a, s, b, op0, op1):
                return dve.scalar_tensor_tensor(out, a, s, b, op0, op1)

            def norm(l, i, gain):
                dve.wait_ge(norm_a.sem, norm_a.after(l, i, "rt"))
                dve.reciprocal(NR[:, :], NR[:, :]).then_inc(norm_v.sem, 1)
                dve.wait_ge(norm_v.sem, norm_v.after(l, i, "ri"))
                for k in range(KT):
                    stt(H[:, k, 0:T], X[:, k, :], gain(k), NR[:, :], ALU.mult, ALU.mult).then_inc(norm_v.sem, 1)

            def ffn(l, f, q0):
                alone(dve)
                with dve.Fori(0, FT // 2) as j:
                    for b in range(2):
                        t = 2 * j + b
                        dve.wait_ge(silu_a.sem, silu_a.after(l, f * FT + t, "silu"))
                        dve.wait_ge(gemm.sem, tile_after(l, q0 + t, 1))
                        tt(mid2[:, bass.ds(2 * t, 2), :], two(gsil[b]), bank2(2 * b + 1, T // 2), ALU.mult
                           ).then_inc(mul_v.sem, 1)
                with dve.Fori(0, KT // 4) as j:
                    for b in range(4):
                        m = 4 * j + b
                        dve.wait_ge(down_p.sem, down_p.after(l, f * KT + m, "down"))
                        x = X2[:, bass.ds(2 * m, 2), :]
                        stt(x, bank2(b, T // 2), 0.5, x, ALU.mult, ALU.add).then_inc(xdone.sem, 1)

            def lora(l):
                for i in range(2):
                    dve.wait_ge(lora_g.sem, lora_g.after(l, 0, f"d{i}2"))
                    stt(D3[:, i, :], D3[:, i, :], P("mu", 24 + i), Y3[:, i, 1:1 + T], ALU.mult, ALU.add
                        ).then_inc(lora_v.sem, 1)

            def glu(l):
                dve.wait_ge(zero_g.sem, zero_g.after(l, 0, "up"))
                dve.wait_ge(mix_load, l * 16 + 16)
                alone(dve)
                h = T // 2
                with dve.Fori(0, CT // 2) as j:
                    for b in range(2):
                        c = 2 * j + b
                        dve.wait_ge(gemm.sem, tile_after(l, Q_CONV + c, 0))
                        dve.wait_ge(glu_a.sem, glu_a.after(l, c, "sig"))
                        g = CG[b].unsqueeze(1)
                        tt(UP[:, bass.ds(c, 1), HIST:HIST + h], PS[:, 4 * b:4 * b + 1, 0:h], g[:, :, 0:h], ALU.mult
                           ).then_inc(glu_v.sem, 1)
                        tt(UP[:, bass.ds(c, 1), HIST + h:HIST + TP], PS[:, 4 * b + 1:4 * b + 2, 0:TP - h],
                           g[:, :, h:TP], ALU.mult).then_inc(glu_v.sem, 1)
                        tt(US[:, bass.ds(c, 1), :, HIST:].rearrange("p a b t -> p (a b) t"),
                           PS[:, 4 * b + 1, TP - h:h].rearrange("p (b t) -> p b t", b=NB),
                           CG[b][:, TP:T].rearrange("p (b t) -> p b t", b=NB), ALU.mult).then_inc(glu_v.sem, 1)

            def dws(c):
                return DW[:, c, TP:T].rearrange("p (b t) -> p b t", b=NB)

            def first_tap(l):
                dve.wait_ge(glu_v.sem, glu_v.after(l, CT - 1, "us"))
                for c in range(CT):
                    w, b = P("conv_w", c * CW), P("conv_b", c)
                    dve.tensor_scalar(DW[:, c, 0:TP], UP[:, c, 0:TP], w, b, ALU.mult, ALU.add).then_inc(tap_v.sem, 1)
                    dve.tensor_scalar(dws(c), US[:, c, :, 0:NT], w, b, ALU.mult, ALU.add).then_inc(tap_v.sem, 1)

            def tap(l, k):
                for c in range(CT):
                    w = P("conv_w", k + c * CW)
                    dve.wait_ge(tap_v.sem, tap_v.after(l, k - 1, f"p{c}"))
                    stt(DW[:, c, 0:TP], UP[:, c, bass.ds(k, TP)], w, DW[:, c, 0:TP], ALU.mult, ALU.add
                        ).then_inc(tap_v.sem, 1)
                    dve.wait_ge(tap_v.sem, tap_v.after(l, k - 1, f"s{c}"))
                    stt(dws(c), US[:, c, :, bass.ds(k, NT)], w, dws(c), ALU.mult, ALU.add).then_inc(tap_v.sem, 1)

            def conv_centre(l):
                dve.wait_ge(cln_p.sem, cln_p.after(l, 0, "mean"))
                for c in range(CT):
                    stt(two(DW[:, c, :]), bank2(0, T // 2), -1.0 / DC, two(DW[:, c, :]), ALU.mult, ALU.add
                        ).then_inc(cln_v.sem, 1)

            def conv_scale(l):
                dve.wait_ge(cln_a.sem, cln_a.after(l, 0, "rt"))
                dve.reciprocal(NR[:, :], NR[:, :]).then_inc(cln_v.sem, 1)
                dve.wait_ge(cln_v.sem, cln_v.after(l, 0, "ri"))
                for c in range(CT):
                    tt(DW[:, c, :], DW[:, c, :], NR[:, :], ALU.mult).then_inc(cln_v.sem, 1)

            R, Kx, V = (D3[:, i, :] for i in range(3))
            pc = PP[:, 0:TP].rearrange("p (c t) -> p c t", c=NC)
            kc = KK[:, 0:TP].rearrange("p (c t) -> p c t", c=NC)
            rc = R[:, 0:TP].rearrange("p (c t) -> p c t", c=NC)

            def mix(l, p, i):
                dve.wait_ge(fg.sem, fg.after(l, p, f"d{i}2"))
                stt(D3[:, i, :], D3[:, i, :], P("mu", p + 8 * i), Y3[:, i, 1:1 + T], ALU.mult, ALU.add
                    ).then_inc(fv.sem, 1)

            def log_decay(l, p):
                dve.wait_ge(fa.sem, fa.after(l, p, "lw"))
                dve.tensor_tensor_scan(CC[:, 0:TP], scan_keep, LW[:, 0:TP], 0.0, ALU.mult, ALU.add
                                       ).then_inc(fv.sem, 1)

            def rate(l, p):
                dve.wait_ge(fa.sem, fa.after(l, p, "a"))
                dve.tensor_scalar(T1, A, P("k_a", p), P("k_a", p), ALU.mult, ALU.subtract).then_inc(fv.sem, 1)

            def key_scale(l, p):
                dve.wait_ge(fa.sem, fa.after(l, p, "rtk"))
                dve.tensor_scalar(KQ, KQ, 1e-12, None, ALU.max).then_inc(fv.sem, 1)
                dve.wait_ge(fv.sem, fv.after(l, p, "inv0"))
                dve.reciprocal(KQ, KQ).then_inc(fv.sem, 1)
                dve.wait_ge(fv.sem, fv.after(l, p, "inv"))
                stt(KK, Kx, P("k_k", p), KQ, ALU.mult, ALU.mult).then_inc(fv.sem, 1)

            def keys(l, p):
                stt(KP, T1, 1.0, Kx, ALU.add, ALU.mult).then_inc(fv.sem, 1)
                dve.wait_ge(fv.sem, fv.after(l, p, "kk"))
                stt(A, KK, -1.0, A, ALU.mult, ALU.mult).then_inc(fv.sem, 1)
                dve.wait_ge(fv.sem, fv.after(l, p, "kp"))
                stt(T1, R, P("r_k", p), KP, ALU.mult, ALU.mult).then_inc(fv.sem, 1)

            def against(l, p):
                dve.wait_ge(fa.sem, fa.after(l, p, "ip"))
                dve.wait_ge(fv.sem, fv.after(l, p, "b"))
                tt(slots(BK)[:, :, 0:4:3, :], tokens(A), tokens(CC), ALU.mult).then_inc(fv.sem, 1)
                tt(slots(BK)[:, :, 1:3, :], tokens(KP), tokens(CC), ALU.mult).then_inc(fv.sem, 1)

            def along(l, p):
                dve.wait_ge(bp.sem, bp.after(l, p - 1, f"y_{NC - 1}"))
                dve.wait_ge(bv.sem, bv.after(l, p - 1, f"sh_{NC - 1}"))
                dve.tensor_copy(PEND.unsqueeze(2), pc[:, :, C - 1:C]).then_inc(fv.sem, 1)
                tt(AR[:, :, 1:C], kc[:, :, 1:C], pc[:, :, 0:C - 1], ALU.mult).then_inc(fv.sem, 1)
                dve.tensor_copy(AR[:, :, 0:1], kc[:, :, 0:1]).then_inc(fv.sem, 1)
                tt(AR[:, :, C:], rc, pc, ALU.mult).then_inc(fv.sem, 1)

            def hat(l, p):
                dve.wait_ge(fv.sem, fv.after(l, p, "bk_k"))
                tt(BKH, BK, pc[:, :, C - 1:C].broadcast_to([128, NC, 128]), ALU.mult).then_inc(fv.sem, 1)

            def bonus(l, p):
                dve.wait_ge(fp.sem, fp.after(l, p, "bon"))
                tt(two(BON), bank2(0, T // 2), two(V), ALU.mult).then_inc(fv.sem, 1)

            def masked(l, p):
                for h in range(2):
                    dve.wait_ge(fp.sem, fp.after(l, p, f"g{h}"))
                    g = PS[:, 6 - 6 * h:8 - 6 * h, :].rearrange("p a (c t) -> p (a c) t", t=128)
                    tt(GM[:, h], g, mask8.unsqueeze(1).broadcast_to([128, NC, 128]), ALU.mult).then_inc(fv.sem, 1)
                tt(GG, GT, GA, ALU.mult).then_inc(fv.sem, 1)

            def flat(x):
                return x.rearrange("p a b c -> p (a b c)")

            def level(l, p, i):
                if i == 0:
                    dve.wait_ge(bg.sem, bg.after(l, p, "ml0"))
                    for q in range(2):
                        r = slice(64 * q, 64 * q + 64)
                        tt(U[r], ML[0][r, :, q::2, :],
                           ident[r, r].unsqueeze(1).unsqueeze(1).broadcast_to([64, 2, NC // 2, C]), ALU.add
                           ).then_inc(bv.sem, 1)
                    return
                dve.wait_ge(bp.sem, bp.after(l, p, f"t{i}" if i < LEVELS - 1 else f"z{i}"))
                tt(flat(U), PS[:, 6, :], flat(U), ALU.add).then_inc(bv.sem, 1)
                if i < LEVELS - 1:
                    if i == 1:
                        dve.wait_ge(ba.sem, ba.after(l, p, "x0"))
                    tt(flat(XI), PS[:, 7, :], flat(XI), ALU.add).then_inc(bv.sem, 1)

            def chunk(l, p, c):
                r = slice(64 * (c % 2), 64 * (c % 2) + 64)
                dve.wait_ge(bp.sem, bp.after(l, p, f"sa_{c}"))
                if c == 0:
                    dve.wait_ge(fa.sem, fa.after(l, p, "tz"))
                dve.tensor_copy(W[r, c, :], PS[r, 5, 0:128]).then_inc(bv.sem, 1)
                dve.wait_ge(bp.sem, bp.after(l, p, f"s_{c}"))
                for h in range(2):
                    hr = slice(64 * h, 64 * h + 64)
                    now = S0[hr, h * N:h * N + N]
                    new = now if c < NC - 1 else STO[hr, bass.ds(p, 1), :].rearrange("p a b -> p (a b)")
                    if c == 0:
                        dve.tensor_copy(new, PS[hr, 6, 0:N]).then_inc(bv.sem, 1)
                    else:
                        stt(new, now, PEND[hr, c:c + 1], PS[hr, 6, 0:N], ALU.mult, ALU.add).then_inc(bv.sem, 1)

            def head_centre(l, p):
                dve.wait_ge(bp.sem, bp.after(l, p, "mean"))
                stt(YO, PS[:, 4, :], -1.0 / N, YO, ALU.mult, ALU.add).then_inc(bv.sem, 1)

            def head_scale(l, p):
                dve.wait_ge(ba.sem, ba.after(l, p, "rt"))
                dve.reciprocal(SQ, SQ).then_inc(bv.sem, 1)
                dve.wait_ge(bv.sem, bv.after(l, p, "ri"))
                tt(YO, YO, SQ, ALU.mult).then_inc(bv.sem, 1)
                dve.wait_ge(bv.sem, bv.after(l, p, "gn"))
                dve.tensor_scalar(YO, YO, P("ln_x_g", p), P("ln_x_b", p), ALU.mult, ALU.add).then_inc(bv.sem, 1)
                dve.wait_ge(bv.sem, bv.after(l, p, "gnb"))
                tt(YO, YO, BON[:, 0:TP], ALU.add).then_inc(bv.sem, 1)
                dve.wait_ge(bv.sem, bv.after(l, p, "ob"))
                tt(Z[:, bass.ds(p, 1), 0:TP].rearrange("p a t -> p (a t)"), YO, GG[:, 0:TP], ALU.mult
                   ).then_inc(bv.sem, 1)

            def first_pair(l):
                mix(l, 0, 0)
                mix(l, 0, 1)
                log_decay(l, 0)
                mix(l, 0, 2)
                rate(l, 0)
                key_scale(l, 0)
                keys(l, 0)
                against(l, 0)
                along(l, 0)
                hat(l, 0)
                bonus(l, 0)
                masked(l, 0)

            def step_of_pairs(l, p):
                n = p + 1
                for i in range(LEVELS):
                    level(l, p, i)
                    if 1 <= i <= 4:
                        tap(l, 4 * p + i)
                    if i == 4:
                        mix(l, n, 0)
                for c in range(NC):
                    chunk(l, p, c)
                    if c == 1:
                        mix(l, n, 1)
                    if c == 2:
                        log_decay(l, n)
                    if c == 4:
                        mix(l, n, 2)
                        rate(l, n)
                    if c == 5:
                        key_scale(l, n)
                    if c == 6:
                        keys(l, n)
                against(l, n)
                along(l, n)
                head_centre(l, p)
                hat(l, n)
                head_scale(l, p)
                bonus(l, n)
                masked(l, n)

            def last_pair(l):
                p = PAIRS - 1
                for i in range(LEVELS):
                    level(l, p, i)
                    if 1 <= i <= 2:
                        tap(l, CW - 3 + i)
                    if i == 4:
                        conv_centre(l)
                for c in range(NC):
                    chunk(l, p, c)
                    if c == 3:
                        conv_scale(l)
                head_centre(l, p)
                head_scale(l, p)

            def over_values(i, t):
                return QT[:, i, bass.ds(t, 1), :].broadcast_to([128, N, N])

            def over_keys(v):
                return v.unsqueeze(2).broadcast_to([128, N, N])

            def scan_step(l, t):
                dve.wait_ge(sp_v.sem, sp_v.after(l, t - 1, "v"))
                tt(M1, SS, over_values(3, t), ALU.mult).then_inc(sp_v.sem, 1)
                dve.wait_ge(sp_v.sem, sp_v.after(l, t, "m"))
                dve.tensor_reduce(SA, M1, AX.X, ALU.add).then_inc(sp_v.sem, 1)
                dve.wait_ge(sp_v.sem, sp_v.after(l, t, "sa"))
                tt(M1, over_keys(SA), over_values(4, t), ALU.mult).then_inc(sp_v.sem, 1)
                dve.wait_ge(sp_v.sem, sp_v.after(l, t, "u"))
                dve.wait_ge(sp_g.sem, sp_g.after(l, t, "sw"))
                tt(SS, SS, M1, ALU.add).then_inc(sp_v.sem, 1)
                dve.wait_ge(sp_v.sem, sp_v.after(l, t, "o"))
                dve.wait_ge(sp_g.sem, sp_g.after(l, t, "vk"))
                tt(SS, SS, M2, ALU.add).then_inc(sp_v.sem, 1)
                dve.wait_ge(sp_v.sem, sp_v.after(l, t, "v"))
                tt(M1, SS, over_values(5, t), ALU.mult).then_inc(sp_v.sem, 1)
                dve.wait_ge(sp_v.sem, sp_v.after(l, t, "y"))
                dve.tensor_reduce(SY[:, bass.ds(t, 1), :].rearrange("p a b -> p (a b)"), M1, AX.X, ALU.add
                                  ).then_inc(sp_v.sem, 1)

            def late(l, m, b):
                z = Z[:, bass.ds(m, 1), :].rearrange("p a t -> p (a t)")
                dve.wait_ge(gemm.sem, tile_after(l, Q_LATE + m, 1))
                dve.wait_ge(late_a.sem, late_a.after(l, m, "gb"))
                tt(two(OB[b]), bank2(2 * b + 1, T // 2), two(GB[b]), ALU.mult).then_inc(late_v.sem, 1)
                dve.wait_ge(late_v.sem, late_v.after(l, m, "ob"))
                tt(z[:, 0:TP], z[:, 0:TP], OB[b][:, 0:TP], ALU.add).then_inc(late_v.sem, 1)
                dve.tensor_copy(z[:, TP:T], OB[b][:, TP:T]).then_inc(late_v.sem, 1)

            def sample_out(l):
                def across(name):
                    return par_sb[:, COL[name]:COL[name] + PAIRS].unsqueeze(2).broadcast_to([128, PAIRS, TS])

                def step(name, out, a, b, op):
                    if name:
                        dve.wait_ge(spo_v.sem, spo_v.after(l, 0, name))
                    tt(out, a, b, op).then_inc(spo_v.sem, 1)
                mean = PS[:, 2, 0:PAIRS * TS].rearrange("p (a t) -> p a t", a=PAIRS)
                dve.wait_ge(sp_p.sem, sp_p.after(l, 0, "mean"))
                stt(YF, mean, -1.0 / N, YF, ALU.mult, ALU.add).then_inc(spo_v.sem, 1)
                dve.wait_ge(sp_a.sem, sp_a.after(l, 0, "rt"))
                dve.reciprocal(YR, YR).then_inc(spo_v.sem, 1)
                step("ri", YF, YF, YR, ALU.mult)
                step("gn", YF, YF, across("ln_x_g"), ALU.mult)
                step("g", YF, YF, across("ln_x_b"), ALU.add)
                step("b", YF, YF, SX[:, :, 0, :], ALU.add)
                step("ob", YF, YF, SX[:, :, 1, :], ALU.mult)
                step("og", YF, YF, SX[:, :, 2, :], ALU.mult)
                dve.wait_ge(late_v.sem, late_v.after(l, KT - 1, "zs"))
                step("oa", Z[:, :, TP:T], Z[:, :, TP:T], YF, ALU.add)

            def mix_out(l):
                alone(dve)
                with dve.Fori(0, KT // 4) as j:
                    for b in range(4):
                        m = 4 * j + b
                        dve.wait_ge(gemm.sem, tile_after(l, Q_OUT + 2 * j + b // 2, b % 2))
                        x = X2[:, bass.ds(2 * m, 2), :]
                        tt(x, bank2(b, T // 2), x, ALU.add).then_inc(xdone.sem, 1)

            with dve.Fori(0, L) as l:
                dve.wait_ge(par_load, l * 16 + 16)
                norm(l, 0, lambda k: P("ffn1_norm", k))
                ffn(l, 0, Q_FFN1)
                norm(l, 1, lambda k: P("mix_norm", k))
                dve.tensor_copy(H[:, :, T:TH], shf_sb[:, bass.ds(l, 1), :, :].rearrange("p a k b -> p (a k) b")
                                ).then_inc(prev_v.sem, 1)
                dve.wait_ge(norm_v.sem, norm_v.after(l, 1, f"h{KT - 1}"))
                dve.tensor_copy(sho[:, bass.ds(l, 1), :, 0:1].rearrange("p a k b -> p (a k) b"),
                                H[:, :, TP - 1:TP]).then_inc(prev_v.sem, 1)
                dve.tensor_copy(sho[:, bass.ds(l, 1), :, 1:].rearrange("p a k b -> p (a k) b"),
                                H[:, :, TP + NT - 1:T:NT]).then_inc(prev_v.sem, 1)
                lora(l)
                glu(l)
                first_tap(l)
                first_pair(l)
                with dve.Fori(0, PAIRS - 1) as p:
                    step_of_pairs(l, p)
                last_pair(l)
                dve.wait_ge(q_got, l * NB * 16 + NB * 16)
                dve.wait_ge(s_load, l * 16 + 16)
                alone(dve)
                with dve.Fori(0, NT) as t:
                    scan_step(l, t)
                    for b in range(2):
                        late(l, 2 * t + b, b)
                sample_out(l)
                mix_out(l)
                norm(l, 2, lambda k: P("ffn2_norm", k))
                ffn(l, 1, Q_FFN2)
            norm(L, 0, lambda k: fn_sb[:, k:k + 1])


def constants():
    k = np.zeros((128, K_ALL), np.float32)
    row, col = np.arange(128)[:, None], np.arange(128)[None, :]
    s, t = np.arange(128)[:, None] % 64, np.arange(64)[None, :]
    k[:, K_ID:K_ID + 128] = row == col
    k[:, K_ONE:K_ONE + 128] = 1
    k[:, K_BLK:K_BLK + 128] = row // 64 == col // 64
    k[:, K_MASK:K_MASK + 64] = s < t
    k[:, K_MASK + 64:K_MASK + 128] = s <= t
    for i in range(LEVELS):
        b = 1 << i
        k[:, K_LEV + 64 * i:K_LEV + 64 * i + 64] = (s // (2 * b) == t // (2 * b)) & (s % (2 * b) < b) & (t % (2 * b) >= b)
    k[:, K_SCAN:K_SCAN + TP] = np.arange(TP)[None, :] % C != 0
    k[:, K_EPS], k[:, K_EPS + 1], k[:, K_EPS + 2] = NORM_EPS, GN_EPS, LN_EPS
    return k


def kernel(**inputs):
    import concourse.bacc as bacc
    from concourse.bass_utils import run_bass_kernel_spmd

    a = {k: np.asarray(v) for k, v in inputs.items()}
    x = np.concatenate([a["x_prompt"].reshape(TP, D), a["x_sample"].reshape(TS, D)])

    def tiles(w, cols):
        part = w[:, cols * 128:cols * 128 + 128]
        return part.reshape(-1, 128, 128).transpose(1, 0, 2).reshape(128, -1)

    def both(u, v):
        return np.concatenate([u, v], axis=1)

    wr, wpa, wpb, wl, wd = [], [], [], [], []
    for l in range(L):
        win = a["w_in"][l]

        def ffn(f):
            wr.extend(both(tiles(a[f + "_w_gate"][l], t), tiles(a[f + "_w_up"][l], t)) for t in range(FT))
            wd.extend(tiles(a[f + "_w_down"][l], m) for m in range(KT))
        ffn("ffn1")
        wr.append(both(tiles(win, 24), tiles(win, 25)))
        wr.extend(both(tiles(win, 26 + c), tiles(win, 30 + c)) for c in range(CT))
        for p in range(PAIRS):
            cols = slice(p * 128, p * 128 + 128)
            wpa.append(both(tiles(win, p), tiles(win, 8 + p)))
            low = np.concatenate([a["w_decay_up"][l][:, cols], a["w_iclr_up"][l][:, cols]])
            wpb.append(np.concatenate([tiles(win, 16 + p), tiles(win, 34 + p), low, a["w_gate_up"][l][:, cols]], axis=1))
        wl.extend(both(tiles(win, 42 + m), tiles(a["w_conv_out"][l], m)) for m in range(KT))
        wr.extend(both(tiles(a["w_out"][l], 2 * i), tiles(a["w_out"][l], 2 * i + 1)) for i in range(KT // 2))
        ffn("ffn2")
    par = []
    for name, n in PARAMS:
        if name == "conv_w":
            par.append(a[name].reshape(L, CW, CT, 128).transpose(0, 3, 2, 1).reshape(L, 128, n))
        else:
            par.append(a[name].reshape(L, n, 128).transpose(0, 2, 1))
    hist = a["state_conv"].reshape(L, NB, HIST, CT, 128).transpose(0, 4, 3, 1, 2)
    hist = np.concatenate([hist, np.zeros((L, 128, CT, NB, NT), np.float32)], axis=-1)
    arrays = {
        "xt": x.reshape(T, KT, 128).transpose(2, 1, 0),
        "par": np.concatenate(par, axis=2),
        "fnorm": a["final_norm"].reshape(KT, 128).T,
        "shf": a["state_shift"].reshape(L, NB, KT, 128).transpose(3, 0, 2, 1),
        "cs": hist.reshape(L, 128, -1),
        "s_in": a["state_wkv"].reshape(L, NB * NH, N * N),
        "wr": np.stack(wr), "wpa": np.stack(wpa), "wpb": np.stack(wpb), "wl": np.stack(wl), "wd": np.stack(wd),
        "consts": constants(),
    }
    arrays = {k: np.ascontiguousarray(v) for k, v in arrays.items()}
    outs = {"y": (128, KT, T), "wkvp": (L, 128, PAIRS * C), "shift": (128, L, KT, 1 + NB),
            "convp": (L, 128, CT, HIST), "wkvs": (L, 128, N * N), "convs": (L, 128, CT * NB * (HIST + NT))}
    nc = bacc.Bacc("TRN2", target_bir_lowering=False, num_devices=1)
    args = [nc.dram_tensor(k, v.shape, F32, kind="ExternalInput").ap() for k, v in arrays.items()]
    args += [nc.dram_tensor("out_" + k, s, F32, kind="ExternalOutput").ap() for k, s in outs.items()]
    build(nc, *args)
    r = run_bass_kernel_spmd(nc, [arrays], core_ids=[0]).results[0]
    got = {k: np.asarray(r["out_" + k]) for k in outs}
    y = got["y"].transpose(2, 1, 0).reshape(T, D)
    shift = got["shift"].transpose(1, 3, 2, 0).reshape(L, 1 + NB, D)
    wkvp = got["wkvp"].reshape(L, 2, N, PAIRS, C).transpose(0, 3, 1, 4, 2).reshape(L, 1, NH, N, N)
    convs = got["convs"].reshape(L, 128, CT, NB, HIST + NT)[..., NT:].transpose(0, 3, 4, 2, 1)
    return (y[:TP].reshape(1, TP, D), y[TP:].reshape(NB, NT, D), wkvp, shift[:, :1],
            got["convp"].transpose(0, 3, 2, 1).reshape(L, 1, HIST, DC),
            got["wkvs"].reshape(L, NB, NH, N, N), shift[:, 1:], convs.reshape(L, NB, HIST, DC))
```

```python
from contextlib import ExitStack

import numpy as np

import concourse.bass as bass
import concourse.mybir as mybir
from concourse.alu_op_type import AluOpType as ALU

F32 = mybir.dt.float32
F32R = mybir.dt.float32r
ACT = mybir.ActivationFunctionType
AX = mybir.AxisListType

L = 2
D = 1024
KT = D // 128
TP = 512
NB, NT = 8, 4
TS = NB * NT
T = TP + TS
TH = T + NB
N = 64
NH = D // N
DFF = 2816
FT = DFF // 128
DC = 512
CT = DC // 128
CW = 31
HIST = CW - 1
C = 64
NC = TP // C
PAIRS = NH // 2
LEVELS = 6
KAPPA = float(np.exp(-0.5))
NORM_EPS, GN_EPS, LN_EPS = 1e-6, 64e-5, 1e-5

PARAMS = [("ffn1_norm", 8), ("mix_norm", 8), ("ffn2_norm", 8), ("mu", 26), ("w0", 8), ("a0", 8),
          ("k_k", 8), ("k_a", 8), ("r_k", 8), ("ln_x_g", 8), ("ln_x_b", 8), ("conv_b", 4),
          ("conv_ln_g", 4), ("conv_ln_b", 4), ("conv_w", CT * CW)]
COL = {}
_at = 0
for _name, _n in PARAMS:
    COL[_name] = _at
    _at += _n
NPAR = _at

Q_FFN1 = 0
Q_LORA = Q_FFN1 + FT
Q_CONV = Q_LORA + 1
Q_PAIR = Q_CONV + CT
Q_LATE = Q_PAIR + 2 * PAIRS
Q_OUT = Q_LATE + KT
Q_FFN2 = Q_OUT + KT // 2
Q_ALL = Q_FFN2 + FT
WR_ALL = Q_ALL - 2 * PAIRS - KT
K_ID, K_ONE, K_BLK, K_MASK, K_LEV, K_I64, K_SCAN = 0, 128, 256, 384, 512, 896, 960
K_EPS = K_SCAN + TP
K_ALL = K_EPS + 4


class Steps:

    def __init__(self, sem, units, names, credit=2):
        self.sem, self.units, self.names, self.credit = sem, units, list(names), credit

    def after(self, l, unit, name):
        n = len(self.names)
        return (l * self.units + unit + self.credit) * n + self.names.index(name) + 1


def build(nc, xt, par, fnorm, shf, cs, s_in, wr, wpa, wpb, wl, wd, consts,
          y_out, wkvp_out, shift_out, convp_out, wkvs_out, convs_out):
    ctx = ExitStack()
    with ctx:
        def sb(name, shape):
            return ctx.enter_context(nc.sbuf_tensor(name, shape, F32))

        def sem(name):
            return ctx.enter_context(nc.semaphore(name))

        scr_q = nc.dram_tensor("scr_q", [6 * TS, D], F32).ap()
        scr_y = nc.dram_tensor("scr_y", [NB * NH, NT * N], F32).ap()

        X = sb("X", [128, KT, T])

        def shared_names(*tensors):
            with ExitStack() as names:
                return [names.enter_context(nc.sbuf_tensor(n, s, *(dt or (F32R,)))) for n, s, *dt in tensors]

        H_hi, = shared_names(("H_hi", [128, KT, TH]))
        H = sb("H", [128, KT, TH])
        ring_mem, W_lo = [], []
        for i in range(2):
            W_lo += shared_names((f"W_lo{i}", [128, 2, KT, 128]))
            ring_mem.append(sb(f"ring{i}", [128, 2 * D + 256]))
        ring = [r[:, 0:2 * D].rearrange("p (a k m) -> p a k m", a=2, k=KT) for r in ring_mem]
        par_sb = sb("par_sb", [128, NPAR])
        fn_sb = sb("fn_sb", [128, KT])
        shf_sb = sb("shf_sb", [128, L, KT, NB])
        sho = sb("sho", [128, L, KT, 1 + NB])
        K = sb("K", [128, K_ALL])
        NR = sb("NR", [128, T])
        mid_hi, mid_lo, H_lo, W_hi0, W_hi1 = shared_names(
            ("mid_hi", [128, FT, T]), ("mid_lo", [128, FT, T]), ("H_lo", [128, KT, T]),
            ("W_hi0", [128, 2, KT, 128]), ("W_hi1", [128, 2, KT, 128]))
        W_hi = [W_hi0, W_hi1]
        (_, D_lo1, D_hi0, D_hi1, gated, D_lo0) = shared_names(
            ("mids", [128, 2 * FT * T]), ("D_lo1", [128, FT, 128]), ("D_hi0", [128, FT, 128]),
            ("D_hi1", [128, FT, 128]), ("gated", [128, 2, T], F32), ("D_lo0", [128, FT, 128]))
        D_hi, D_lo = [D_hi0, D_hi1], [D_lo0, D_lo1]
        arena = sb("arena", [128, 36896])
        PS = ctx.enter_context(nc.psum_tensor("PS", [128, 8, 512], F32))

        ident, ones, blk = (K[:, a:a + 128] for a in (K_ID, K_ONE, K_BLK))
        mask8 = K[:, K_MASK:K_MASK + 128]
        lev = K[:, K_LEV:K_LEV + LEVELS * C].rearrange("p (l t) -> p l t", l=LEVELS)
        i64 = K[:, K_I64:K_I64 + C]
        scan_keep = K[:, K_SCAN:K_SCAN + TP]
        eps_norm, eps_gn, eps_ln = (K[:, K_EPS + i:K_EPS + i + 1] for i in range(3))

        def P(name, i=0):
            return par_sb[:, bass.ds(COL[name] + i, 1)]

        class Take:
            def __init__(self, start):
                self.at = start

            def __call__(self, *dims):
                n = int(np.prod(dims))
                v = arena[:, self.at:self.at + n]
                self.at += n
                assert self.at <= 36896, self.at
                if len(dims) == 1:
                    return v
                names = "abcd"[:len(dims)]
                return v.rearrange(f"p ({' '.join(names)}) -> p {' '.join(names)}",
                                   **{k: d for k, d in zip(names, dims)})

        take = Take(0)
        take(2 * FT * T)
        H_raw = Take(take.at)(KT, T)
        second_down = take(FT, 128)
        take(2 * FT * 128)
        take(2 * T)
        gsil = [gated[:, i, :] for i in range(2)]
        dring = [take(FT, 128), second_down]
        take = Take(0)
        Z = take(KT, T)
        xwa, sg = take(T), take(T)
        UP = take(CT, HIST + TP)
        US = take(CT, NB, HIST + NT)
        DW = take(CT, T)
        SQT = take(PAIRS, 6, TS)
        SX = take(PAIRS, 3, TS)
        shared = take.at
        Y3 = take(3, TH + 1)
        D3 = take(3, T)
        LW, A, PP, KQ, KK, KP = (take(T) for _ in range(6))
        BK, BKH, ZV = (take(NC, 128) for _ in range(3))
        T1, GT, GA = take(T), take(T), take(T)
        in_use = take.at
        CC, GG, BON = take(T), take(T), take(T)
        PEND = take(NC)
        AR, BKT, W = (take(NC, 128) for _ in range(3))
        GM = take(2, NC, 128)
        ML = [take(2, NC, C) for _ in range(2)]
        U, XI, AS = (take(2, NC // 2, C) for _ in range(3))
        S0, XS, YO = take(128), take(128), take(TP)
        SQ = CC[:, 0:TP]
        STO = take(PAIRS, C)
        take = Take(shared)
        SS = take(N, N)
        QT = take(6, NT, N)
        QA, QB = take(D), take(D)
        GB, OB = [take(T) for _ in range(2)], [take(T) for _ in range(2)]
        LQ = GB + OB
        assert take.at <= in_use
        take = Take(in_use)
        M1, M2 = take(N, N), take(N, N)
        SA, SY, YT = take(N), take(NT, N), take(D)
        YF, YR = take(PAIRS, TS), take(PAIRS, TS)

        CG = [KK, KP]

        def slots(x):
            return x.rearrange("p (e q) (s t) -> p e (q s) t", q=2, s=2)

        def tokens(x):
            return x[:, 0:TP].rearrange("p (e q t) -> p e q t", q=2, t=C)

        def bank2(s, n):
            return PS[:, 2 * s:2 * s + 2, 0:n]

        def two(a):
            return a.rearrange("p (a b) -> p a b", a=2)

        const_load, par_load, x_load = sem("const_load"), sem("par_load"), sem("x_load")
        ring_load = [[sem(f"ring_load{i}_{half}") for half in range(2)] for i in range(2)]
        d_load = [sem(f"d_load{i}") for i in range(2)]
        mix_load, s_load = sem("mix_load"), sem("s_load")
        out_done, conv_out_done = sem("out_done"), sem("conv_out_done")
        q_put, q_got, y_put, y_got, s_out = (sem(n) for n in ("q_put", "q_got", "y_put", "y_got", "s_out"))

        gemm = Steps(sem("gemm_done"), 2 * Q_ALL, ["tile"], 4)
        xdone = Steps(sem("x_updated"), 3, [f"m{m}" for m in range(KT)], 1)
        norm_a = Steps(sem("norm_act"), 3, [f"sq{k}" for k in range(KT)] + ["rt"])
        norm_p = Steps(sem("norm_pe"), 3, ["ss"])
        norm_v = Steps(sem("norm_dve"), 3, ["ri"] + [f"h{k}" for k in range(KT)])
        prev_v = Steps(sem("shift_dve"), 1, ["prev", "out0", "out1"])
        hhi_a = Steps(sem("h_hi_act"), 2, [f"k{k}" for k in range(KT)])
        hlo_g = Steps(sem("h_lo_pool"), 2, [f"k{k}" for k in range(3)])
        hlo_v = Steps(sem("h_lo_dve"), 2, [f"k{k}" for k in range(3, KT)])
        whi_a = Steps(sem("w_hi_act"), 2 * FT, ["gate", "up"])
        wlo_v = Steps(sem("w_lo_dve"), 2 * FT, ["gate", "up"])
        mhi_a = Steps(sem("mid_hi_act"), 2 * FT, ["hi"])
        mlo_v = Steps(sem("mid_lo_dve"), 2 * FT, ["lo"])
        dhi_a = Steps(sem("d_hi_act"), 2 * KT, ["p0", "p1"])
        dlo_v = Steps(sem("d_lo_dve"), 2 * KT, ["p0", "p1"])
        silu_a = Steps(sem("ffn_silu"), 2 * FT, ["silu"])
        mul_v = Steps(sem("ffn_mul"), 2 * FT, ["mul"])
        down_p = Steps(sem("down_pe"), 2 * KT, ["down"])
        lora_a = Steps(sem("lora_act"), 1, ["y0", "y1", "tanh", "xa", "sg"])
        lora_g = Steps(sem("lora_pool"), 1, [f"d{i}{j}" for i in range(2) for j in range(3)])
        lora_v = Steps(sem("lora_dve"), 1, ["x0", "x1"])
        glu_a = Steps(sem("glu_act"), CT, ["sig"])
        glu_v = Steps(sem("glu_dve"), CT, ["u0", "u1", "us"])
        tap_v = Steps(sem("conv_tap"), CW, [f"{s}{c}" for c in range(CT) for s in "ps"])
        cln_p = Steps(sem("conv_ln_pe"), 1, ["mean", "var"])
        cln_a = Steps(sem("conv_ln_act"), 1, [f"sq{c}" for c in range(CT)] + ["rt"] + [f"out{c}" for c in range(CT)])
        cln_v = Steps(sem("conv_ln_dve"), 1, [f"dc{c}" for c in range(CT)] + ["ri"] + [f"n{c}" for c in range(CT)])
        fp = Steps(sem("front_pe"), PAIRS, ["kk", "dec", "gate", "icl", "g0", "tb", "g1", "tz", "bon"])
        fa = Steps(sem("front_act"), PAIRS, ["y0", "sqk", "rtk", "y1", "lw", "y2", "gt", "a", "p", "ip",
                                             "pw", "zv", "ga", "tb", "tz"])
        fg = Steps(sem("front_pool"), PAIRS, [f"d{i}{j}" for i in range(3) for j in range(3)]
                   + ["s_kk", "s_r", "s_v", "s_kp", "s_b", "s_gt", "s_ga"])
        kv = Steps(sem("key_row_dve"), PAIRS, ["x0"])
        fv = Steps(sem("front_dve"), PAIRS, ["inv0", "inv", "kk", "x1", "c", "x2", "t1", "kp", "b",
                                             "bk_b", "bk_k", "pend", "ar_a", "ar_0", "ar_r", "hat", "rk",
                                             "g0", "g1", "bon", "gg"])
        bon_g = Steps(sem("bonus_pool"), PAIRS, ["s"])
        hp = Steps(sem("head_norm_pe"), PAIRS, ["mean", "var"])
        ha = Steps(sem("head_norm_act"), PAIRS, ["sq", "rt"])
        hv = Steps(sem("head_norm_dve"), PAIRS, ["dc", "ri", "gn", "gnb", "ob", "z"])
        bp = Steps(sem("back_pe"), PAIRS, ["x0"] + [f"{s}{i}" for i in range(1, LEVELS) for s in "azt"][:-1]
                   + [f"{s}_{c}" for c in range(NC) for s in ("x", "sa", "s", "y")])
        bg = Steps(sem("back_pool"), PAIRS, [f"ml{i}" for i in range(1, LEVELS)])
        bv = Steps(sem("back_dve"), PAIRS,
                   ["m0l", "m0", "u0"] + [f"{s}{i}" for i in range(1, LEVELS) for s in "ux"][:-1]
                   + [f"{s}_{c}" for c in range(NC) for s in ("sa", "sl", "sh")])
        ba = Steps(sem("back_act"), PAIRS, ["x0"] + [f"a{i}" for i in range(1, LEVELS)]
                   + [f"{s}_{c}" for c in range(NC) for s in ("xs", "y")])
        late_a = Steps(sem("late_act"), KT, ["gb"])
        late_v = Steps(sem("late_dve"), KT, ["ob"])
        late_g = Steps(sem("late_pool"), KT, ["zp", "zs"])
        zero_g = Steps(sem("zeros_pool"), 1, ["y", "up", "zv", "s0"])
        sp_p = Steps(sem("sample_pe"), 1, ["tq0", "tq1", "ty", "mean", "var"])
        sp_a = Steps(sem("sample_act"), 1, ["qa", "qb", "yf", "sq", "rt"])
        SCAN = ["m", "sa", "u", "o", "v", "y", "r"]
        sp_v = Steps(sem("sample_dve"), NT, SCAN)
        sp_g = Steps(sem("sample_pool"), NT, ["vk", "sw"])
        spo_v = Steps(sem("sample_out"), 1, ["dc", "ri", "gn", "g", "b", "ob", "og", "oa", "z"])
        ALL_STEPS = {
            "pe": [gemm, norm_p, down_p, cln_p, fp, bp, hp, sp_p],
            "act": [norm_a, hhi_a, whi_a, mhi_a, dhi_a, silu_a, lora_a, glu_a, cln_a, fa, ba, ha, late_a, sp_a],
            "dve": [xdone, norm_v, hlo_v, wlo_v, mlo_v, dlo_v, prev_v, mul_v, lora_v, glu_v, tap_v, cln_v, kv, fv, bv, hv, late_v, sp_v, spo_v],
            "pool": [hlo_g, lora_g, fg, bg, bon_g, late_g, sp_g, zero_g],
        }

        waits_met = sem("waits_met")

        def grant(eng, which):
            for s in ALL_STEPS[which]:
                eng.sem_inc(s.sem, len(s.names) * s.credit)

        def alone(eng):
            eng.sem_inc(waits_met, 1)

        def tile_after(l, q, half):
            return gemm.after(l, 2 * q + half, "tile")

        RING_N = [(Q_ALL - i + 1) // 2 for i in range(2)]

        def ring_value(l, q0, j=0):
            return (l * RING_N[q0 % 2] + q0 // 2 + j + 1) * 16

        HALF = FT // 2

        block = ctx.enter_context(nc.Block())

        @block.sync
        def _(sp):
            sp.dma_start(K[:, :], consts).then_inc(const_load, 16)
            sp.dma_start(X[:, :, :], xt).then_inc(x_load, 16)
            sp.dma_start(fn_sb[:, :], fnorm).then_inc(const_load, 16)
            sp.dma_start(shf_sb[:, :, :, :], shf).then_inc(const_load, 16)

            def load_ring(l, q0, j, src):
                q = q0 + 2 * j
                n = src.shape[-1]
                for half, cols in enumerate((slice(0, D), slice(D, n))):
                    sp.wait_ge(gemm.sem, tile_after(l, q - 2, half))
                    sp.dma_start(ring_mem[q0 % 2][:, cols], src[:, cols]).then_inc(ring_load[q0 % 2][half], 16)

            def row(w, i):
                return w[bass.ds(i, 1)].rearrange("a p n -> p (a n)")

            def wr_at(l, i):
                return row(wr, l * WR_ALL + i)

            def load_down(l, f, b, j):
                sp.dma_start(dring[b].rearrange("p k m -> p (k m)"),
                             wd[bass.ds(l * 2 * KT + f * KT + 2 * j + b, 1)].rearrange("a p n -> p (a n)")
                             ).then_inc(d_load[b], 16)

            def ffn_loads(l, f, q0, i0):
                alone(sp)
                with sp.Fori(0, FT // 2) as j:
                    for b in range(2):
                        load_ring(l, q0 + b, j, wr_at(l, i0 + b + 2 * j))
                for b in range(2):
                    if b == 0:
                        sp.wait_ge(down_p.sem, down_p.after(l, f * KT - 2, "down"))
                    else:
                        sp.wait_ge(gemm.sem, tile_after(l, q0 + FT - 1, 1))
                    alone(sp)
                    load_down(l, f, b, 0)
                alone(sp)
                with sp.Fori(1, KT // 2) as j:
                    for b in range(2):
                        sp.wait_ge(down_p.sem, down_p.after(l, f * KT + 2 * j + b - 2, "down"))
                        load_down(l, f, b, j)

            with sp.Fori(0, L) as l:
                sp.wait_ge(xdone.sem, xdone.after(l, -1, f"m{KT - 1}"))
                sp.dma_start(par_sb[:, :], par[bass.ds(l, 1)].rearrange("a p n -> p (a n)")).then_inc(par_load, 16)
                ffn_loads(l, 0, Q_FFN1, 0)
                load_ring(l, Q_LORA, 0, wr_at(l, Q_LORA))
                sp.wait_ge(xdone.sem, xdone.after(l, 0, f"m{KT - 1}"))
                sp.dma_start(US.rearrange("p a b c -> p (a b c)"),
                             cs[bass.ds(l, 1)].rearrange("a p n -> p (a n)")).then_inc(mix_load, 16)
                with sp.Fori(0, CT // 2) as j:
                    for b in range(2):
                        load_ring(l, Q_CONV + b, j, wr_at(l, Q_CONV + b + 2 * j))
                sp.wait_ge(zero_g.sem, zero_g.after(l, 0, "zv"))
                sp.wait_ge(glu_v.sem, glu_v.after(l, CT - 1, "us"))
                sp.dma_start(convp_out[bass.ds(l, 1)].rearrange("a p c n -> p (a c) n"),
                             UP[:, :, TP:TP + HIST]).then_inc(conv_out_done, 16)
                sp.dma_start(convs_out[bass.ds(l, 1)].rearrange("a p n -> p (a n)"),
                             US.rearrange("p a b c -> p (a b c)")).then_inc(conv_out_done, 16)
                with sp.Fori(0, PAIRS) as p:
                    load_ring(l, Q_PAIR, p, row(wpa, l * PAIRS + p))
                    load_ring(l, Q_PAIR + 1, p, row(wpb, l * PAIRS + p))
                def load_late(j):
                    for b in range(2):
                        load_ring(l, Q_LATE + b, j, wl[bass.ds(l * KT + b + 2 * j, 1)].rearrange("a p n -> p (a n)"))
                alone(sp)
                load_late(0)
                by_q = scr_q.rearrange("(b q t) n -> q b t n", b=NB, q=6)
                for i in range(6):
                    if i == 0:
                        sp.wait_ge(sp_a.sem, sp_a.after(l, 0, "qa"))
                    if i == 4:
                        sp.wait_ge(sp_a.sem, sp_a.after(l, 0, "qb"))
                    rows = QA[TS * i:TS * i + TS] if i < 4 else QB[TS * (i - 4):TS * (i - 4) + TS]
                    sp.dma_start(by_q[i], rows).then_inc(q_put, 16)
                sp.wait_ge(fv.sem, fv.after(l, PAIRS - 1, "gg"))
                alone(sp)
                sp.dma_start(SS.rearrange("p a b -> p (a b)"),
                             s_in[bass.ds(l, 1)].rearrange("a p n -> p (a n)")).then_inc(s_load, 16)
                sp.wait_ge(q_put, l * 96 + 96)
                for b in range(NB):
                    sp.dma_start(QT[b * NH:(b + 1) * NH].rearrange("h q t j -> h (q t) j"),
                                 scr_q.rearrange("(b q t) (h j) -> b h (q t) j", b=NB, q=6, h=NH)[b]
                                 ).then_inc(q_got, 16)
                sp.wait_ge(bv.sem, bv.after(l, PAIRS - 1, f"sh_{NC - 1}"))
                alone(sp)
                sp.dma_start(wkvp_out[bass.ds(l, 1)].rearrange("a p n -> p (a n)"),
                             STO.rearrange("p a b -> p (a b)")).then_inc(s_out, 16)
                with sp.Fori(1, KT // 2) as j:
                    load_late(j)
                sp.wait_ge(sp_v.sem, sp_v.after(l, NT - 1, "r"))
                sp.dma_start(scr_y, SY.rearrange("p t j -> p (t j)")).then_inc(y_put, 16)
                sp.dma_start(wkvs_out[bass.ds(l, 1)].rearrange("a p n -> p (a n)"),
                             SS.rearrange("p a b -> p (a b)")).then_inc(s_out, 16)
                sp.wait_ge(y_put, l * 16 + 16)
                for b in range(NB):
                    sp.dma_start(YT[b * NT:(b + 1) * NT].rearrange("t (h j) -> t h j", h=NH),
                                 scr_y.rearrange("(b h) (t j) -> b t h j", b=NB, t=NT)[b]).then_inc(y_got, 16)
                sp.wait_ge(conv_out_done, l * 32 + 32)
                sp.wait_ge(s_out, l * 32 + 32)
                alone(sp)
                with sp.Fori(0, KT // 4) as j:
                    for b in range(2):
                        load_ring(l, Q_OUT + b, j, wr_at(l, Q_PAIR + b + 2 * j))
                ffn_loads(l, 1, Q_FFN2, Q_PAIR + KT // 2)
            sp.wait_ge(prev_v.sem, prev_v.after(L - 1, 0, "out1"))
            sp.dma_start(shift_out, sho[:, :, :, :]).then_inc(out_done, 16)
            sp.wait_ge(norm_v.sem, norm_v.after(L, 0, f"h{KT - 1}"))
            sp.dma_start(y_out, H[:, :, 0:T]).then_inc(out_done, 16)
            sp.wait_ge(out_done, 32)

        @block.gpsimd
        def _(pool):
            grant(pool, "pool")

            def diff(l, steps, unit, i, y, d):
                ys = y[:, 1 + TP:1 + T].rearrange("p (b t) -> p b t", b=NB)
                ds = d[:, TP:T].rearrange("p (b t) -> p b t", b=NB)
                pool.tensor_tensor(d[:, 0:TP], y[:, 0:TP], y[:, 1:1 + TP], ALU.subtract).then_inc(steps.sem, 1)
                pool.tensor_tensor(ds[:, :, 1:NT], ys[:, :, 0:NT - 1], ys[:, :, 1:NT], ALU.subtract
                                   ).then_inc(steps.sem, 1)
                pool.tensor_tensor(ds[:, :, 0], y[:, 1 + T:1 + TH], ys[:, :, 0], ALU.subtract
                                   ).then_inc(steps.sem, 1)

            def level(l, p, i):
                if i == 1:
                    pool.wait_ge(fv.sem, fv.after(l, p, "g1"))
                if i >= 3:
                    pool.wait_ge(bp.sem, bp.after(l, p, f"a{i - 2}"))
                m = lev[:, i, :].unsqueeze(1).unsqueeze(1).broadcast_to([128, 2, NC, C])
                pool.tensor_tensor(ML[i % 2], GM[:, :, :, 0:C], m, ALU.mult).then_inc(bg.sem, 1)

            def shift(l, p, i):
                pool.wait_ge(fa.sem, fa.after(l, p, f"y{i}"))
                if i == 2:
                    pool.wait_ge(fv.sem, fv.after(l, p - 1, "bon"))
                diff(l, fg, p, i, Y3[:, i, :], D3[:, i, :])

            def keep(l, p, ready, name, done, dst, src):
                pool.wait_ge(ready.sem, ready.after(l, p, name))
                alone(pool)
                pool.tensor_copy(dst.rearrange("p a t -> p (a t)"), src[:, TP:T]).then_inc(done.sem, 1)

            def keeps(l, p):
                keep(l, p, fv, "kk", fg, SQT[:, bass.ds(p, 1), 3, :], KK)
                keep(l, p, fv, "x1", fg, SQT[:, bass.ds(p, 1), 5, :], D3[:, 1, :])
                keep(l, p, fv, "x2", fg, SQT[:, bass.ds(p, 1), 2, :], D3[:, 2, :])
                keep(l, p, fv, "kp", fg, SQT[:, bass.ds(p, 1), 1, :], KP)
                keep(l, p, fv, "b", fg, SQT[:, bass.ds(p, 1), 4, :], A)
                keep(l, p, fa, "gt", fg, SX[:, bass.ds(p, 1), 1, :], GT)
                keep(l, p, fa, "ga", fg, SX[:, bass.ds(p, 1), 2, :], GA)

            def keep_bonus(l, p):
                keep(l, p, fv, "bon", bon_g, SX[:, bass.ds(p, 1), 0, :], BON)

            def first_pair(l):
                for i in range(3):
                    shift(l, 0, i)
                keeps(l, 0)

            def step_of_pairs(l, p):
                for i in range(1, 4):
                    level(l, p, i)
                shift(l, p + 1, 0)
                for i in (4, 5):
                    level(l, p, i)
                keep_bonus(l, p)
                for i in (1, 2):
                    shift(l, p + 1, i)
                keeps(l, p + 1)

            def last_pair(l):
                for i in range(1, LEVELS):
                    level(l, PAIRS - 1, i)
                keep_bonus(l, PAIRS - 1)

            def outer(l, t):
                pool.wait_ge(sp_v.sem, sp_v.after(l, t - 1, "v"))
                pool.tensor_tensor(M2, QT[:, 2, bass.ds(t, 1), :].rearrange("p a n -> p n a").broadcast_to([128, N, N]),
                                   QT[:, 1, bass.ds(t, 1), :].broadcast_to([128, N, N]), ALU.mult
                                   ).then_inc(sp_g.sem, 1)

            def decayed(l, t):
                pool.wait_ge(sp_v.sem, sp_v.after(l, t, "m"))
                pool.tensor_tensor(SS, SS, QT[:, 0, bass.ds(t, 1), :].broadcast_to([128, N, N]), ALU.mult
                                   ).then_inc(sp_g.sem, 1)

            def late(l, m, b):
                z = Z[:, bass.ds(m, 1), :].rearrange("p a t -> p (a t)")
                pool.wait_ge(late_v.sem, late_v.after(l, m, "ob"))
                pool.tensor_tensor(z[:, 0:TP], z[:, 0:TP], OB[b][:, 0:TP], ALU.add).then_inc(late_g.sem, 1)
                pool.tensor_copy(z[:, TP:T], OB[b][:, TP:T]).then_inc(late_g.sem, 1)

            def ffn_rows(l, f):
                for k in range(3):
                    pool.wait_ge(hhi_a.sem, hhi_a.after(l, f, f"k{k}"))
                    pool.tensor_tensor(H_lo[:, k, :], H_raw[:, k, :], H_hi[:, k, 0:T], ALU.subtract).then_inc(hlo_g.sem, 1)

            with pool.Fori(0, L) as l:
                ffn_rows(l, 0)
                pool.wait_ge(xdone.sem, xdone.after(l, 0, f"m{KT - 1}"))
                alone(pool)
                pool.memset(Y3[:, :, 0:1], 0.0).then_inc(zero_g.sem, 1)
                pool.memset(UP[:, :, 0:HIST], 0.0).then_inc(zero_g.sem, 1)
                pool.memset(slots(ZV)[:, :, 0:4:3, :], 0.0).then_inc(zero_g.sem, 1)
                pool.memset(S0, 0.0).then_inc(zero_g.sem, 1)
                for i in range(2):
                    pool.wait_ge(lora_a.sem, lora_a.after(l, 0, f"y{i}"))
                    pool.wait_ge(zero_g.sem, zero_g.after(l, 0, "y"))
                    diff(l, lora_g, 0, i, Y3[:, i, :], D3[:, i, :])
                first_pair(l)
                with pool.Fori(0, PAIRS - 1) as p:
                    step_of_pairs(l, p)
                last_pair(l)
                pool.wait_ge(q_got, l * NB * 16 + NB * 16)
                pool.wait_ge(hv.sem, hv.after(l, PAIRS - 1, "z"))
                alone(pool)
                outer(l, 0)
                with pool.Fori(0, NT - 1) as t:
                    decayed(l, t)
                    outer(l, t + 1)
                    for b in range(2):
                        late(l, 2 * t + b, b)
                decayed(l, NT - 1)
                for b in range(2):
                    late(l, KT - 2 + b, b)
                ffn_rows(l, 1)

        @block.tensor
        def _(pe):
            grant(pe, "pe")

            def tile(out, w, rhs, n, kt=KT):
                for half in range(2):
                    for k in range(kt):
                        last = pe.matmul(out[:, half, :], w[:, k, :], rhs[:, k, half * n:half * n + n],
                                         start=(k == 0), stop=(k == kt - 1))
                return last

            def norm(l, i):
                pe.wait_ge(xdone.sem, xdone.after(l, i - 1, "m4"))
                for k in range(KT):
                    pe.wait_ge(norm_a.sem, norm_a.after(l, i, f"sq{k}"))
                    for half in range(2):
                        last = pe.matmul(bank2(0, T // 2)[:, half, :], ones, H[:, k, half * T // 2:half * T // 2 + T // 2],
                                         start=(k == 0), stop=(k == KT - 1), skip_group_check=True)
                last.then_inc(norm_p.sem, 1)

            def split_tile(out, w_hi, w_lo, x_hi, x_lo, ks, kt):
                n = T // 2
                for k in ks:
                    for half in range(2):
                        cols = slice(half * n, half * n + n)
                        pe.matmul(out[:, half, :], w_hi[:, k, :], x_hi[:, k, cols],
                                  start=(k == 0), stop=False, skip_group_check=True)
                    for half in range(2):
                        cols = slice(half * n, half * n + n)
                        pe.matmul(out[:, half, :], w_hi[:, k, :], x_lo[:, k, cols],
                                  start=False, stop=False, skip_group_check=True)
                    for half in range(2):
                        cols = slice(half * n, half * n + n)
                        last = pe.matmul(out[:, half, :], w_lo[:, k, :], x_hi[:, k, cols],
                                         start=False, stop=(k == kt - 1), skip_group_check=True)
                return last

            def ffn(l, f, q0):
                def gate_up(j, b, first=False):
                    t = f * FT + 2 * j + b
                    s = (q0 + b) % 2
                    pe.wait_ge(wlo_v.sem, wlo_v.after(l, t, "gate"))
                    pe.wait_ge(silu_a.sem, silu_a.after(l, t - 2, "silu"))
                    for k in range(KT):
                        if first and k < 3:
                            pe.wait_ge(hlo_g.sem, hlo_g.after(l, f, f"k{k}"))
                        elif first:
                            pe.wait_ge(hlo_v.sem, hlo_v.after(l, f, f"k{k}"))
                        last = split_tile(bank2(2 * b, T // 2), W_hi[s][:, 0], W_lo[s][:, 0], H_hi, H_lo, [k], KT)
                    last.then_inc(gemm.sem, 1)
                    pe.wait_ge(wlo_v.sem, wlo_v.after(l, t, "up"))
                    pe.wait_ge(mul_v.sem, mul_v.after(l, t - 2, "mul"))
                    split_tile(bank2(2 * b + 1, T // 2), W_hi[s][:, 1], W_lo[s][:, 1], H_hi, H_lo, range(KT), KT
                               ).then_inc(gemm.sem, 1)
                gate_up(0, 0, first=True)
                gate_up(0, 1)
                alone(pe)
                with pe.Fori(1, FT // 2) as j:
                    for b in range(2):
                        gate_up(j, b)
                alone(pe)
                with pe.Fori(0, KT // 4) as j:
                    for b in range(4):
                        m = 4 * j + b
                        pe.wait_ge(xdone.sem, xdone.after(l, 2 * f, "m0") + m - 4)
                        for h in range(2):
                            pe.wait_ge(mlo_v.sem, mlo_v.after(l, f * FT + (HALF, FT)[h] - 1, "lo"))
                            pe.wait_ge(dlo_v.sem, dlo_v.after(l, f * KT + m, f"p{h}"))
                            last = split_tile(bank2(b, T // 2), D_hi[b % 2], D_lo[b % 2], mid_hi, mid_lo,
                                              range(h * HALF, h * HALF + HALF), FT)
                        last.then_inc(down_p.sem, 1)

            def lora(l):
                pe.wait_ge(prev_v.sem, prev_v.after(l, 0, "prev"))
                for half in range(2):
                    pe.wait_ge(ring_load[Q_LORA % 2][half], ring_value(l, Q_LORA))
                n = TH // 2
                for i in range(2):
                    for k in range(KT):
                        if i == 0:
                            pe.wait_ge(norm_v.sem, norm_v.after(l, 1, f"h{k}"))
                        for half in range(2):
                            last = pe.matmul(bank2(i, n)[:, half, :], ring[Q_LORA % 2][:, i, k, :],
                                             H[:, k, half * n:half * n + n], start=(k == 0), stop=(k == KT - 1),
                                             skip_group_check=True)
                    last.then_inc(gemm.sem, 1)

            def conv_in(l):
                alone(pe)
                with pe.Fori(0, CT // 2) as j:
                    for b in range(2):
                        q = Q_CONV + b
                        for half in range(2):
                            pe.wait_ge(ring_load[q % 2][half], ring_value(l, q, j))
                        if b == 0:
                            pe.wait_ge(lora_a.sem, lora_a.after(l, 0, "y1"))
                        pe.wait_ge(glu_v.sem, glu_v.after(l, 2 * j + b - 2, "us"))
                        tile(bank2(2 * b, T // 2), ring[q % 2][:, 0], H, T // 2).then_inc(gemm.sem, 1)
                        pe.wait_ge(glu_a.sem, glu_a.after(l, 2 * j + b - 2, "sig"))
                        tile(bank2(2 * b + 1, T // 2), ring[q % 2][:, 1], H, T // 2).then_inc(gemm.sem, 1)

            def over_channels(l, steps, name, slot, x):
                for c in range(CT):
                    pe.wait_ge(steps.sem, steps.after(l, *name(c)))
                    for half in range(2):
                        last = pe.matmul(bank2(slot, T // 2)[:, half, :], ones, x(c)[:, half * T // 2:half * T // 2 + T // 2],
                                         start=(c == 0), stop=(c == CT - 1), skip_group_check=True)
                last.then_inc(cln_p.sem, 1)

            def conv_mean(l):
                over_channels(l, tap_v, lambda c: (CW - 1, f"s{c}"), 0, lambda c: DW[:, c, :])

            def conv_var(l):
                over_channels(l, cln_a, lambda c: (0, f"sq{c}"), 1, lambda c: LQ[c])

            def wide(out, w, rhs):
                for half in range(2):
                    last = pe.matmul(out[:, half, :], w, rhs[:, half * T // 2:half * T // 2 + T // 2],
                                     start=True, stop=True)
                return last

            F0, F1 = (bank2(i, TH // 2) for i in range(2))
            G0, G1 = (bank2(i, T // 2) for i in range(2))

            def part(l, p, i, k0, k1):
                q = Q_PAIR + i // 2
                out, n = ((F0, TH // 2), (F1, TH // 2), (F0, TH // 2), (G0, T // 2))[i]
                if k0 == 0:
                    if i % 2 == 0:
                        for half in range(2):
                            pe.wait_ge(ring_load[q % 2][half], ring_value(l, q, p))
                    if i == 0:
                        pe.wait_ge(fv.sem, fv.after(l, p - 1, "g1"))
                    elif i == 1:
                        pe.wait_ge(fa.sem, fa.after(l, p - 1, "tb"))
                        pe.wait_ge(ha.sem, ha.after(l, p - 2, "rt"))
                    elif i == 2:
                        pe.wait_ge(fa.sem, fa.after(l, p, "rtk"))
                    else:
                        pe.wait_ge(fa.sem, fa.after(l, p, "a"))
                for k in range(k0, k1):
                    for half in range(2):
                        last = pe.matmul(out[:, half, :], ring[q % 2][:, i % 2, k, :], H[:, k, half * n:half * n + n],
                                         start=(k == 0), stop=(k == KT - 1), skip_group_check=True)
                if k1 == KT:
                    last.then_inc(gemm.sem, 1)

            def low_rank(l, p, name):
                q = (Q_PAIR + 1) % 2
                if name == "dec":
                    for half in range(2):
                        pe.wait_ge(ring_load[q][half], ring_value(l, Q_PAIR + 1, p))
                    pe.wait_ge(fa.sem, fa.after(l, p, "y1"))
                    wide(G1, ring_mem[q][0:64, 2 * D:2 * D + 128], xwa[0:64]).then_inc(fp.sem, 1)
                elif name == "gate":
                    pe.wait_ge(fa.sem, fa.after(l, p, "lw"))
                    wide(G1, ring_mem[q][:, 2 * D + 128:2 * D + 256], sg).then_inc(fp.sem, 1)
                else:
                    pe.wait_ge(fa.sem, fa.after(l, p, "y2"))
                    wide(G0, ring_mem[q][64:128, 2 * D:2 * D + 128], xwa[64:128]).then_inc(fp.sem, 1)

            def key_norm(l, p):
                pe.wait_ge(fv.sem, fv.after(l, p - 1, "bon"))
                pe.wait_ge(fa.sem, fa.after(l, p, "sqk"))
                wide(G0, blk, KQ).then_inc(fp.sem, 1)

            def bonus(l, p):
                pe.wait_ge(fv.sem, fv.after(l, p, "g1"))
                wide(G0, blk, T1).then_inc(fp.sem, 1)

            def gram(l, p, h):
                base = 6 - 6 * h
                for c in range(NC):
                    r = slice(64 * h, 64 * h + 64)
                    last = pe.matmul(PS[:, base + c // 4, (c % 4) * 128:(c % 4) * 128 + 128], BK[r, c, :], AR[r, c, :],
                                     start=True, stop=True)
                last.then_inc(fp.sem, 1)

            def token_major(base, x):
                for c in range(NC):
                    last = pe.transpose(PS[:, base + c // 4, (c % 4) * 128:(c % 4) * 128 + 128], x[:, c, :], ident)
                last.then_inc(fp.sem, 1)

            def head_mean(l, p):
                pe.wait_ge(ba.sem, ba.after(l, p, f"y_{NC - 1}"))
                pe.matmul(PS[:, 2, :], blk, YO, start=True, stop=True).then_inc(hp.sem, 1)

            def head_var(l, p):
                pe.wait_ge(ha.sem, ha.after(l, p, "sq"))
                pe.matmul(PS[:, 3, :], blk, SQ, start=True, stop=True).then_inc(hp.sem, 1)

            def finish(l, p):
                pe.wait_ge(bv.sem, bv.after(l, p - 1, f"sh_{NC - 1}"))
                pe.wait_ge(ba.sem, ba.after(l, p - 1, f"y_{NC - 1}"))
                pe.wait_ge(fv.sem, fv.after(l, p, "ar_r"))
                gram(l, p, 0)
                pe.wait_ge(fa.sem, fa.after(l, p, "ga"))
                pe.wait_ge(fv.sem, fv.after(l, p, "hat"))
                token_major(2, BKH)
                gram(l, p, 1)
                token_major(4, ZV)

            def first_pair(l):
                part(l, 0, 0, 0, KT)
                part(l, 0, 1, 0, KT)
                key_norm(l, 0)
                part(l, 0, 2, 0, KT)
                low_rank(l, 0, "dec")
                low_rank(l, 0, "gate")
                low_rank(l, 0, "icl")
                part(l, 0, 3, 0, KT)
                finish(l, 0)

            def blocks(bank, w, x):
                for h in range(2):
                    for e in range(NC // 2):
                        for q in range(2):
                            r = slice(64 * q, 64 * q + 64)
                            at = (h * (NC // 2) + e) * C
                            last = pe.matmul(PS[r, bank, at:at + C], w[r, h, e if w.shape[2] < NC else 2 * e + q, :],
                                             x[r, r] if x is ident else x[r, h, e, :], start=True, stop=True)
                return last

            def level(l, p, i, fill):
                if i == 0:
                    pe.wait_ge(bv.sem, bv.after(l, p, "u0"))
                    pe.wait_ge(fa.sem, fa.after(l, p, "tz"))
                    alone(pe)
                    blocks(4, U, ident).then_inc(bp.sem, 1)
                    return
                pe.wait_ge(bg.sem, bg.after(l, p, f"ml{i}"))
                if i == 1:
                    pe.wait_ge(ba.sem, ba.after(l, p, "x0"))
                else:
                    pe.wait_ge(bv.sem, bv.after(l, p, f"x{i - 1}"))
                alone(pe)
                blocks(5, ML[i % 2], XI).then_inc(bp.sem, 1)
                fill(0)
                pe.wait_ge(ba.sem, ba.after(l, p, f"a{i}"))
                alone(pe)
                blocks(6, AS, U).then_inc(bp.sem, 1)
                if i < LEVELS - 1:
                    blocks(7, U, AS).then_inc(bp.sem, 1)
                fill(1)

            def chunk(l, p, c, fill):
                q, e = c % 2, c // 2
                r = slice(64 * q, 64 * q + 64)
                if c == 0:
                    pe.wait_ge(bv.sem, bv.after(l, p, f"u{LEVELS - 1}"))
                if c > 0:
                    pe.wait_ge(bv.sem, bv.after(l, p, f"sh_{c - 1}"))
                    pe.matmul(PS[r, 4, 0:128], AR[:, c, 0:C], S0, start=True, stop=False, skip_group_check=True)
                for h in range(2):
                    last = pe.matmul(PS[r, 4, h * N:h * N + N], GM[:, h, c, 0:C], W[:, c, h * N:h * N + N],
                                     start=(c == 0), stop=True, skip_group_check=True)
                last.then_inc(bp.sem, 1)
                if c > 0:
                    pe.wait_ge(ba.sem, ba.after(l, p, f"y_{c - 1}"))
                    pe.matmul(PS[:, 7, 0:C], S0, AR[:, c, C:2 * C], start=True, stop=False, skip_group_check=True)
                fill(0)
                pe.wait_ge(ba.sem, ba.after(l, p, f"xs_{c}"))
                alone(pe)
                for h in range(2):
                    last = pe.matmul(PS[r, 5, h * N:h * N + N], U[r, h, e, :], XS[r, h * N:h * N + N],
                                     start=True, stop=True)
                last.then_inc(bp.sem, 1)
                fill(1)
                pe.wait_ge(bv.sem, bv.after(l, p, f"sa_{c}"))
                for h in range(2):
                    last = pe.matmul(PS[64 * h:64 * h + 64, 6, 0:N], BKT[:, c, h * N:h * N + N], W[:, c, h * N:h * N + N],
                                     start=True, stop=True)
                last.then_inc(bp.sem, 1)
                for h in range(2):
                    last = pe.matmul(PS[64 * h:64 * h + 64, 7, 0:C], W[:, c, h * N:h * N + N], GM[:, h, c, C:2 * C],
                                     start=(c == 0), stop=True, skip_group_check=True)
                last.then_inc(bp.sem, 1)
                fill(2)

            def step_of_pairs(l, p, first=False):
                n = p + 1

                def rows(i):
                    part(l, n, i // KT, i % KT, i % KT + 1)

                rows(0)
                rows(1)
                level(l, p, 0, None)
                if not first:
                    head_mean(l, p - 1)

                def fill_level(i, s):
                    if i == 3 and s == 0:
                        pe.wait_ge(fa.sem, fa.after(l, n, "y0"))
                        bonus(l, p)
                    if i < 4:
                        at = 3 * i - 1
                        rows(at + s)
                        if s == 1:
                            if i == 1 and not first:
                                head_var(l, p - 1)
                            rows(at + 2)
                    elif i == 4:
                        rows(11 + s)
                        if s == 0:
                            key_norm(l, n)
                    else:
                        rows(13 + s)
                        if s == 1:
                            rows(15)
                for i in range(1, LEVELS):
                    level(l, p, i, lambda s: fill_level(i, s))

                def fill_chunk(c, s):
                    at = 3 * c + s
                    if at < 3:
                        part(l, n, 2, at, at + 1)
                    elif at == 3:
                        low_rank(l, n, "dec")
                    elif at < 9:
                        part(l, n, 2, at - 1, at)
                    elif at == 9:
                        low_rank(l, n, "gate")
                    elif at == 10:
                        low_rank(l, n, "icl")
                    elif 12 <= at < 20:
                        part(l, n, 3, at - 12, at - 11)
                for c in range(NC):
                    chunk(l, p, c, lambda s: fill_chunk(c, s))
                finish(l, n)

            def samples(l, g):
                if g == 0:
                    pe.wait_ge(fg.sem, fg.after(l, PAIRS - 1, "s_ga"))
                rows = (128, 64)[g]
                alone(pe)
                for p in range(PAIRS):
                    last = pe.transpose(PS[0:rows, 2 * g + p // 4, (p % 4) * 128:(p % 4) * 128 + 128],
                                        SQT[:, p, 4 * g:4 * g + rows // TS, :].rearrange("p a t -> p (a t)"), ident)
                last.then_inc(sp_p.sem, 1)

            def last_pair(l):
                p = PAIRS - 1
                for i in range(LEVELS):
                    level(l, p, i, lambda s: None)
                    if i == 0:
                        head_mean(l, p - 1)
                        samples(l, 0)
                    if i == 1:
                        head_var(l, p - 1)
                    if i == 2:
                        pe.wait_ge(sp_a.sem, sp_a.after(l, 0, "qa"))
                        bonus(l, p)
                    if i == 3:
                        pe.wait_ge(ha.sem, ha.after(l, p - 1, "rt"))
                        samples(l, 1)
                    if i == 4:
                        pe.wait_ge(fv.sem, fv.after(l, p, "bon"))
                        conv_mean(l)
                for c in range(NC):
                    chunk(l, p, c, lambda s: None)
                    if c == 1:
                        pe.wait_ge(sp_a.sem, sp_a.after(l, 0, "qb"))
                        conv_var(l)
                pe.wait_ge(cln_a.sem, cln_a.after(l, 0, "rt"))
                head_mean(l, p)
                head_var(l, p)

            def late(l):
                pe.wait_ge(cln_a.sem, cln_a.after(l, 0, f"out{CT - 1}"))
                pe.wait_ge(ha.sem, ha.after(l, PAIRS - 1, "rt"))
                alone(pe)
                with pe.Fori(0, KT // 2) as j:
                    for b in range(2):
                        q = Q_LATE + b
                        for half in range(2):
                            pe.wait_ge(ring_load[q % 2][half], ring_value(l, q, j))
                        pe.wait_ge(late_a.sem, late_a.after(l, 2 * j + b - 2, "gb"))
                        tile(bank2(2 * b, T // 2), ring[q % 2][:, 0], H, T // 2).then_inc(gemm.sem, 1)
                        pe.wait_ge(late_v.sem, late_v.after(l, 2 * j + b - 2, "ob"))
                        tile(bank2(2 * b + 1, T // 2), ring[q % 2][:, 1], DW, T // 2, CT).then_inc(gemm.sem, 1)
                pe.wait_ge(y_got, l * NB * 16 + NB * 16)
                pe.wait_ge(late_a.sem, late_a.after(l, KT - 1, "gb"))
                pe.wait_ge(late_v.sem, late_v.after(l, KT - 1, "ob"))
                alone(pe)
                for p in range(PAIRS):
                    last = pe.transpose(PS[:, 0, p * TS:(p + 1) * TS], YT[0:TS, p * 128:(p + 1) * 128], ident[0:TS, 0:TS])
                last.then_inc(sp_p.sem, 1)
                pe.wait_ge(sp_a.sem, sp_a.after(l, 0, "yf"))
                pe.matmul(PS[:, 2, 0:PAIRS * TS], blk, YF.rearrange("p a t -> p (a t)"), start=True, stop=True
                          ).then_inc(sp_p.sem, 1)
                pe.wait_ge(sp_a.sem, sp_a.after(l, 0, "sq"))
                pe.matmul(PS[:, 4, 0:PAIRS * TS], blk, YR.rearrange("p a t -> p (a t)"), start=True, stop=True
                          ).then_inc(sp_p.sem, 1)

            def mix_out(l):
                pe.wait_ge(spo_v.sem, spo_v.after(l, 0, "z"))
                alone(pe)
                with pe.Fori(0, KT // 4) as j:
                    for b in range(4):
                        q = Q_OUT + b // 2
                        for half in range(2):
                            pe.wait_ge(ring_load[q % 2][half], ring_value(l, q, j))
                        pe.wait_ge(xdone.sem, xdone.after(l, 1, "m0") + 4 * j + b - 4)
                        tile(bank2(b, T // 2), ring[q % 2][:, b % 2], Z, T // 2).then_inc(gemm.sem, 1)

            pe.wait_ge(const_load, 48)
            with pe.Fori(0, L) as l:
                norm(l, 0)
                ffn(l, 0, Q_FFN1)
                norm(l, 1)
                lora(l)
                conv_in(l)
                pe.wait_ge(lora_a.sem, lora_a.after(l, 0, "sg"))
                pe.wait_ge(glu_v.sem, glu_v.after(l, CT - 1, "us"))
                pe.wait_ge(mix_load, l * 16 + 16)
                first_pair(l)
                step_of_pairs(l, 0, first=True)
                alone(pe)
                with pe.Fori(1, PAIRS - 1) as p:
                    step_of_pairs(l, p)
                last_pair(l)
                late(l)
                mix_out(l)
                norm(l, 2)
                ffn(l, 1, Q_FFN2)
            norm(L, 0)

        @block.scalar
        def _(act):
            grant(act, "act")

            def norm(l, i):
                for k in range(KT):
                    act.wait_ge(xdone.sem, xdone.after(l, i - 1, f"m{k}"))
                    act.activation(H[:, k, 0:T], X[:, k, :], ACT.Square).then_inc(norm_a.sem, 1)
                if i % 2 == 0 and l is not L:
                    split_weights(l, i // 2, (Q_FFN1, Q_FFN2)[i // 2], 0, 0, 0)
                act.wait_ge(norm_p.sem, norm_p.after(l, i, "ss"))
                act.activation(two(NR[:, :]), bank2(0, T // 2), ACT.Sqrt, scale=1.0 / D, bias=eps_norm
                               ).then_inc(norm_a.sem, 1)

            def split_weights(l, f, q0, j, b, u):
                s = (q0 + b) % 2
                act.wait_ge(ring_load[s][u], ring_value(l, q0 + b, j))
                act.activation(W_hi[s][:, u], ring[s][:, u], ACT.Copy).then_inc(whi_a.sem, 1)

            def split_down(l, f, b, j, halves=range(2)):
                act.wait_ge(d_load[b], ((l * 2 + f) * (KT // 2) + j + 1) * 16)
                for h in halves:
                    ks = slice(h * HALF, h * HALF + HALF)
                    act.activation(D_hi[b][:, ks], dring[b][:, ks], ACT.Copy).then_inc(dhi_a.sem, 1)

            def ffn(l, f, q0):
                split_weights(l, f, q0, 0, 0, 1)
                for k in range(KT):
                    act.wait_ge(norm_v.sem, norm_v.after(l, 2 * f, f"h{k}"))
                    act.activation(H_hi[:, k, 0:T], H_raw[:, k, :], ACT.Copy).then_inc(hhi_a.sem, 1)

                def silu(t, b):
                    act.wait_ge(gemm.sem, tile_after(l, q0 + t, 0))
                    act.wait_ge(mlo_v.sem, mlo_v.after(l, f * FT + t - 2, "lo"))
                    act.activation(two(gsil[b]), bank2(2 * b, T // 2), ACT.Silu).then_inc(silu_a.sem, 1)

                def mid_high(t, b):
                    act.wait_ge(mul_v.sem, mul_v.after(l, f * FT + t, "mul"))
                    act.activation(mid_hi[:, bass.ds(t, 1), :].rearrange("p a t -> p (a t)"), gsil[b], ACT.Copy
                                   ).then_inc(mhi_a.sem, 1)
                alone(act)
                with act.Fori(0, FT // 2 - 1) as j:
                    for b in range(2):
                        silu(2 * j + b, b)
                        for u in range(2):
                            split_weights(l, f, q0, j + b, 1 - b, u)
                        mid_high(2 * j + b, b)
                silu(FT - 2, 0)
                for u in range(2):
                    split_weights(l, f, q0, FT // 2 - 1, 1, u)
                mid_high(FT - 2, 0)
                silu(FT - 1, 1)
                act.wait_ge(gemm.sem, tile_after(l, q0 + FT - 1, 1))
                split_down(l, f, 0, 0, [0])
                mid_high(FT - 1, 1)
                split_down(l, f, 0, 0, [1])
                alone(act)
                with act.Fori(0, KT // 2 - 1) as j:
                    split_down(l, f, 1, j)
                    split_down(l, f, 0, j + 1)
                split_down(l, f, 1, KT // 2 - 1)

            def lora(l):
                for i in range(2):
                    act.wait_ge(gemm.sem, tile_after(l, Q_LORA, i))
                    act.activation(two(Y3[:, i, 1:1 + TH]), bank2(i, TH // 2), ACT.Copy).then_inc(lora_a.sem, 1)
                act.wait_ge(lora_v.sem, lora_v.after(l, 0, "x0"))
                act.activation(xwa[0:64], D3[0:64, 0, :], ACT.Tanh).then_inc(lora_a.sem, 1)
                act.activation(xwa[64:128], D3[64:128, 0, :], ACT.Copy).then_inc(lora_a.sem, 1)
                act.wait_ge(lora_v.sem, lora_v.after(l, 0, "x1"))
                act.activation(sg, D3[:, 1, :], ACT.Sigmoid).then_inc(lora_a.sem, 1)

            def glu(l):
                alone(act)
                with act.Fori(0, CT // 2) as j:
                    for b in range(2):
                        act.wait_ge(gemm.sem, tile_after(l, Q_CONV + b + 2 * j, 1))
                        act.wait_ge(glu_v.sem, glu_v.after(l, 2 * j + b - 2, "us"))
                        act.activation(two(CG[b]), bank2(2 * b + 1, T // 2), ACT.Sigmoid).then_inc(glu_a.sem, 1)

            def conv_squares(l):
                for c in range(CT):
                    if c == 0:
                        act.wait_ge(fv.sem, fv.after(l, PAIRS - 1, "bon"))
                    act.wait_ge(cln_v.sem, cln_v.after(l, 0, f"dc{c}"))
                    act.activation(LQ[c], DW[:, c, :], ACT.Square).then_inc(cln_a.sem, 1)

            def conv_root(l):
                act.wait_ge(cln_p.sem, cln_p.after(l, 0, "var"))
                act.activation(two(NR[:, :]), bank2(1, T // 2), ACT.Sqrt, scale=1.0 / DC, bias=eps_ln
                               ).then_inc(cln_a.sem, 1)

            def conv_silu(l):
                for c in range(CT):
                    act.wait_ge(cln_v.sem, cln_v.after(l, 0, f"n{c}"))
                    act.activation(DW[:, c, :], DW[:, c, :], ACT.Silu, scale=P("conv_ln_g", c), bias=P("conv_ln_b", c)
                                   ).then_inc(cln_a.sem, 1)

            G0, G1 = (bank2(i, T // 2) for i in range(2))

            def row_out(l, p, i):
                if i == 0:
                    act.wait_ge(fv.sem, fv.after(l, p - 1, "g1"))
                    act.wait_ge(fg.sem, fg.after(l, p - 1, "s_ga"))
                act.wait_ge(gemm.sem, tile_after(l, Q_PAIR + 2 * p + i // 2, i % 2))
                act.activation(two(Y3[:, i, 1:1 + TH]), bank2(i % 2, TH // 2), ACT.Copy).then_inc(fa.sem, 1)

            def decay(l, p):
                act.wait_ge(fp.sem, fp.after(l, p, "dec"))
                act.activation(two(LW), G1, ACT.Sigmoid, bias=P("w0", p)).then_inc(fa.sem, 1)

            def key_squares(l, p):
                act.wait_ge(kv.sem, kv.after(l, p, "x0"))
                act.activation(KQ, D3[:, 0, :], ACT.Square, scale=P("k_k", p)).then_inc(fa.sem, 1)

            def gate_rate(l, p):
                act.wait_ge(fv.sem, fv.after(l, p - 1, "gg"))
                act.wait_ge(fp.sem, fp.after(l, p, "gate"))
                act.activation(two(GT), G1, ACT.Copy).then_inc(fa.sem, 1)
                act.wait_ge(fp.sem, fp.after(l, p, "icl"))
                act.activation(two(A), G0, ACT.Sigmoid, bias=P("a0", p)).then_inc(fa.sem, 1)

            def key_root(l, p):
                act.wait_ge(fp.sem, fp.after(l, p, "kk"))
                act.activation(two(KQ), G0, ACT.Sqrt).then_inc(fa.sem, 1)

            def decays(l, p):
                act.wait_ge(fv.sem, fv.after(l, p, "c"))
                act.activation(PP[:, 0:TP], CC[:, 0:TP], ACT.Exp, scale=-KAPPA).then_inc(fa.sem, 1)
                act.activation(CC[:, 0:TP], CC[:, 0:TP], ACT.Exp, scale=KAPPA).then_inc(fa.sem, 1)
                act.activation(SQT[:, bass.ds(p, 1), 0, :].rearrange("p a t -> p (a t)"), LW[:, TP:T], ACT.Exp,
                               scale=-KAPPA).then_inc(fa.sem, 1)

            def values(l, p):
                act.wait_ge(fv.sem, fv.after(l, p, "x2"))
                act.wait_ge(zero_g.sem, zero_g.after(l, 0, "s0"))
                act.activation(slots(ZV)[:, :, 1:3, :], tokens(D3[:, 2, :]), ACT.Copy).then_inc(fa.sem, 1)

            def gate_a(l, p):
                act.wait_ge(gemm.sem, tile_after(l, Q_PAIR + 2 * p + 1, 1))
                act.activation(two(GA), G0, ACT.Sigmoid).then_inc(fa.sem, 1)

            def transposed(l, p, name, bank, dst):
                act.wait_ge(fp.sem, fp.after(l, p, name))
                act.activation(dst.rearrange("p c n -> p (c n)"), PS[:, bank:bank + 2, :].rearrange("p a b -> p (a b)"), ACT.Copy
                               ).then_inc(fa.sem, 1)

            def flat(x):
                return x.rearrange("p a b c -> p (a b c)")

            def level(l, p, i):
                if i == 0:
                    act.wait_ge(bp.sem, bp.after(l, p, "x0"))
                    act.activation(flat(XI), PS[:, 4, :], ACT.Copy).then_inc(ba.sem, 1)
                else:
                    act.wait_ge(bp.sem, bp.after(l, p, f"a{i}"))
                    act.activation(flat(AS), PS[:, 5, :], ACT.Copy).then_inc(ba.sem, 1)

            def chunk(l, p, c):
                r = slice(64 * (c % 2), 64 * (c % 2) + 64)
                act.wait_ge(bp.sem, bp.after(l, p, f"x_{c}"))
                act.activation(XS[r], PS[r, 4, 0:128], ACT.Copy).then_inc(ba.sem, 1)
                if c == 0:
                    act.wait_ge(hv.sem, hv.after(l, p - 1, "z"))
                act.wait_ge(bp.sem, bp.after(l, p, f"y_{c}"))
                act.activation(YO[:, c * C:c * C + C], PS[:, 7, 0:C], ACT.Copy).then_inc(ba.sem, 1)

            def head_squares(l, p):
                act.wait_ge(hv.sem, hv.after(l, p, "dc"))
                act.activation(SQ, YO, ACT.Square).then_inc(ha.sem, 1)

            def head_root(l, p):
                act.wait_ge(hp.sem, hp.after(l, p, "var"))
                act.activation(SQ, PS[:, 3, :], ACT.Sqrt, scale=1.0 / N, bias=eps_gn).then_inc(ha.sem, 1)

            def first_pair(l):
                row_out(l, 0, 0)
                key_squares(l, 0)
                key_root(l, 0)
                row_out(l, 0, 1)
                decay(l, 0)
                row_out(l, 0, 2)
                gate_rate(l, 0)
                decays(l, 0)
                values(l, 0)
                gate_a(l, 0)
                transposed(l, 0, "tb", 2, BKT)
                transposed(l, 0, "tz", 4, W)

            def step_of_pairs(l, p, first=False):
                n = p + 1
                for i in range(LEVELS):
                    level(l, p, i)
                    if i == 1 and not first:
                        head_squares(l, p - 1)
                    if i == 2:
                        if not first:
                            head_root(l, p - 1)
                        row_out(l, n, 0)
                    if i == 3:
                        key_squares(l, n)
                    if i == 4:
                        key_root(l, n)
                for c in range(NC):
                    chunk(l, p, c)
                    if c == 0:
                        row_out(l, n, 1)
                    if c == 1:
                        decay(l, n)
                    if c == 2:
                        row_out(l, n, 2)
                    if c == 3:
                        gate_rate(l, n)
                    if c == 5:
                        decays(l, n)
                        values(l, n)
                    if c == 6:
                        gate_a(l, n)
                transposed(l, n, "tb", 2, BKT)
                transposed(l, n, "tz", 4, W)

            def last_pair(l):
                p = PAIRS - 1
                for i in range(LEVELS):
                    level(l, p, i)
                    if i == 0:
                        act.wait_ge(sp_p.sem, sp_p.after(l, 0, "tq0"))
                        act.activation(QA, PS[:, 0:2, :].rearrange("p a b -> p (a b)"), ACT.Copy).then_inc(sp_a.sem, 1)
                    if i == 1:
                        head_squares(l, p - 1)
                    if i == 2:
                        head_root(l, p - 1)
                    if i == 4:
                        act.wait_ge(sp_p.sem, sp_p.after(l, 0, "tq1"))
                        act.activation(QB[0:64], PS[0:64, 2:4, :].rearrange("p a b -> p (a b)"), ACT.Copy
                                       ).then_inc(sp_a.sem, 1)
                conv_squares(l)
                for c in range(NC):
                    chunk(l, p, c)
                    if c == 2:
                        conv_root(l)
                    if c == 4:
                        conv_silu(l)
                head_squares(l, p)
                head_root(l, p)

            def late(l):
                alone(act)
                with act.Fori(0, KT // 2) as j:
                    for b in range(2):
                        act.wait_ge(gemm.sem, tile_after(l, Q_LATE + b + 2 * j, 0))
                        act.wait_ge(late_v.sem, late_v.after(l, 2 * j + b - 2, "ob"))
                        act.activation(two(GB[b]), bank2(2 * b, T // 2), ACT.Sigmoid).then_inc(late_a.sem, 1)
                act.wait_ge(sp_p.sem, sp_p.after(l, 0, "ty"))
                act.activation(YF.rearrange("p a t -> p (a t)"), PS[:, 0, 0:PAIRS * TS], ACT.Copy).then_inc(sp_a.sem, 1)
                act.wait_ge(spo_v.sem, spo_v.after(l, 0, "dc"))
                act.activation(YR.rearrange("p a t -> p (a t)"), YF.rearrange("p a t -> p (a t)"), ACT.Square
                               ).then_inc(sp_a.sem, 1)
                act.wait_ge(sp_p.sem, sp_p.after(l, 0, "var"))
                act.activation(YR.rearrange("p a t -> p (a t)"), PS[:, 4, 0:PAIRS * TS], ACT.Sqrt, scale=1.0 / N,
                               bias=eps_gn).then_inc(sp_a.sem, 1)

            act.wait_ge(const_load, 48)
            act.wait_ge(x_load, 16)
            alone(act)
            with act.Fori(0, L) as l:
                norm(l, 0)
                ffn(l, 0, Q_FFN1)
                norm(l, 1)
                lora(l)
                glu(l)
                first_pair(l)
                step_of_pairs(l, 0, first=True)
                alone(act)
                with act.Fori(1, PAIRS - 1) as p:
                    step_of_pairs(l, p)
                last_pair(l)
                late(l)
                norm(l, 2)
                ffn(l, 1, Q_FFN2)
            norm(L, 0)

        @block.vector
        def _(dve):
            grant(dve, "dve")
            X2 = X[:, :, :].rearrange("p t (a b) -> p (t a) b", a=2)

            def tt(out, a, b, op):
                return dve.tensor_tensor(out, a, b, op)

            def stt(out, a, s, b, op0, op1):
                return dve.scalar_tensor_tensor(out, a, s, b, op0, op1)

            def norm(l, i, gain):
                if i % 2 == 0 and l is not L:
                    split_weights(l, i // 2, (Q_FFN1, Q_FFN2)[i // 2], 0, 0, 0)
                rows = H_raw if i % 2 == 0 and l is not L else H
                dve.wait_ge(norm_a.sem, norm_a.after(l, i, "rt"))
                dve.reciprocal(NR[:, :], NR[:, :]).then_inc(norm_v.sem, 1)
                dve.wait_ge(norm_v.sem, norm_v.after(l, i, "ri"))
                for k in range(KT):
                    stt(rows[:, k, 0:T], X[:, k, :], gain(k), NR[:, :], ALU.mult, ALU.mult).then_inc(norm_v.sem, 1)

            def split_weights(l, f, q0, j, b, u):
                s = (q0 + b) % 2
                dve.wait_ge(whi_a.sem, whi_a.after(l, f * FT + 2 * j + b, ("gate", "up")[u]))
                tt(W_lo[s][:, u], ring[s][:, u], W_hi[s][:, u], ALU.subtract).then_inc(wlo_v.sem, 1)

            def split_down(l, f, b, j, halves=range(2)):
                for h in halves:
                    ks = slice(h * HALF, h * HALF + HALF)
                    dve.wait_ge(dhi_a.sem, dhi_a.after(l, f * KT + 2 * j + b, f"p{h}"))
                    tt(D_lo[b][:, ks], dring[b][:, ks], D_hi[b][:, ks], ALU.subtract).then_inc(dlo_v.sem, 1)

            def ffn(l, f, q0):
                for k in range(3, KT):
                    dve.wait_ge(hhi_a.sem, hhi_a.after(l, f, f"k{k}"))
                    tt(H_lo[:, k, :], H_raw[:, k, :], H_hi[:, k, 0:T], ALU.subtract).then_inc(hlo_v.sem, 1)
                split_weights(l, f, q0, 0, 0, 1)

                def product(t, b):
                    dve.wait_ge(silu_a.sem, silu_a.after(l, f * FT + t, "silu"))
                    dve.wait_ge(gemm.sem, tile_after(l, q0 + t, 1))
                    tt(two(gsil[b]), two(gsil[b]), bank2(2 * b + 1, T // 2), ALU.mult).then_inc(mul_v.sem, 1)

                def mid_low(t, b):
                    dve.wait_ge(mhi_a.sem, mhi_a.after(l, f * FT + t, "hi"))
                    at = bass.ds(t, 1)
                    tt(mid_lo[:, at, :].rearrange("p a t -> p (a t)"), gsil[b],
                       mid_hi[:, at, :].rearrange("p a t -> p (a t)"), ALU.subtract).then_inc(mlo_v.sem, 1)

                def update(m, b):
                    dve.wait_ge(down_p.sem, down_p.after(l, f * KT + m, "down"))
                    x = X2[:, bass.ds(2 * m, 2), :]
                    stt(x, bank2(b, T // 2), 0.5, x, ALU.mult, ALU.add).then_inc(xdone.sem, 1)
                alone(dve)
                with dve.Fori(0, FT // 2 - 1) as j:
                    for b in range(2):
                        for u in range(2):
                            split_weights(l, f, q0, j + b, 1 - b, u)
                        product(2 * j + b, b)
                        mid_low(2 * j + b, b)
                for u in range(2):
                    split_weights(l, f, q0, FT // 2 - 1, 1, u)
                product(FT - 2, 0)
                mid_low(FT - 2, 0)
                product(FT - 1, 1)
                split_down(l, f, 0, 0, [0])
                mid_low(FT - 1, 1)
                split_down(l, f, 0, 0, [1])
                for m in range(KT):
                    if m < KT - 1:
                        split_down(l, f, (m + 1) % 2, (m + 1) // 2)
                    update(m, m % 4)

            def lora(l):
                for i in range(2):
                    dve.wait_ge(lora_g.sem, lora_g.after(l, 0, f"d{i}2"))
                    stt(D3[:, i, :], D3[:, i, :], P("mu", 24 + i), Y3[:, i, 1:1 + T], ALU.mult, ALU.add
                        ).then_inc(lora_v.sem, 1)

            def glu(l):
                dve.wait_ge(zero_g.sem, zero_g.after(l, 0, "up"))
                dve.wait_ge(mix_load, l * 16 + 16)
                alone(dve)
                h = T // 2
                with dve.Fori(0, CT // 2) as j:
                    for b in range(2):
                        c = 2 * j + b
                        dve.wait_ge(gemm.sem, tile_after(l, Q_CONV + c, 0))
                        dve.wait_ge(glu_a.sem, glu_a.after(l, c, "sig"))
                        g = CG[b].unsqueeze(1)
                        tt(UP[:, bass.ds(c, 1), HIST:HIST + h], PS[:, 4 * b:4 * b + 1, 0:h], g[:, :, 0:h], ALU.mult
                           ).then_inc(glu_v.sem, 1)
                        tt(UP[:, bass.ds(c, 1), HIST + h:HIST + TP], PS[:, 4 * b + 1:4 * b + 2, 0:TP - h],
                           g[:, :, h:TP], ALU.mult).then_inc(glu_v.sem, 1)
                        tt(US[:, bass.ds(c, 1), :, HIST:].rearrange("p a b t -> p (a b) t"),
                           PS[:, 4 * b + 1, TP - h:h].rearrange("p (b t) -> p b t", b=NB),
                           CG[b][:, TP:T].rearrange("p (b t) -> p b t", b=NB), ALU.mult).then_inc(glu_v.sem, 1)

            def dws(c):
                return DW[:, c, TP:T].rearrange("p (b t) -> p b t", b=NB)

            def first_tap(l):
                dve.wait_ge(glu_v.sem, glu_v.after(l, CT - 1, "us"))
                for c in range(CT):
                    w, b = P("conv_w", c * CW), P("conv_b", c)
                    dve.tensor_scalar(DW[:, c, 0:TP], UP[:, c, 0:TP], w, b, ALU.mult, ALU.add).then_inc(tap_v.sem, 1)
                    dve.tensor_scalar(dws(c), US[:, c, :, 0:NT], w, b, ALU.mult, ALU.add).then_inc(tap_v.sem, 1)

            def tap(l, k, tiles=range(CT)):
                for c in tiles:
                    w = P("conv_w", k + c * CW)
                    dve.wait_ge(tap_v.sem, tap_v.after(l, k - 1, f"p{c}"))
                    stt(DW[:, c, 0:TP], UP[:, c, bass.ds(k, TP)], w, DW[:, c, 0:TP], ALU.mult, ALU.add
                        ).then_inc(tap_v.sem, 1)
                    dve.wait_ge(tap_v.sem, tap_v.after(l, k - 1, f"s{c}"))
                    stt(dws(c), US[:, c, :, bass.ds(k, NT)], w, dws(c), ALU.mult, ALU.add).then_inc(tap_v.sem, 1)

            def conv_centre(l):
                dve.wait_ge(cln_p.sem, cln_p.after(l, 0, "mean"))
                for c in range(CT):
                    stt(two(DW[:, c, :]), bank2(0, T // 2), -1.0 / DC, two(DW[:, c, :]), ALU.mult, ALU.add
                        ).then_inc(cln_v.sem, 1)

            def conv_scale(l):
                dve.wait_ge(cln_a.sem, cln_a.after(l, 0, "rt"))
                dve.reciprocal(NR[:, :], NR[:, :]).then_inc(cln_v.sem, 1)
                dve.wait_ge(cln_v.sem, cln_v.after(l, 0, "ri"))
                for c in range(CT):
                    tt(DW[:, c, :], DW[:, c, :], NR[:, :], ALU.mult).then_inc(cln_v.sem, 1)

            Kx, R, V = (D3[:, i, :] for i in range(3))
            pc = PP[:, 0:TP].rearrange("p (c t) -> p c t", c=NC)
            kc = KK[:, 0:TP].rearrange("p (c t) -> p c t", c=NC)
            rc = R[:, 0:TP].rearrange("p (c t) -> p c t", c=NC)

            def mix(l, p, i):
                dve.wait_ge(fg.sem, fg.after(l, p, f"d{i}2"))
                stt(D3[:, i, :], D3[:, i, :], P("mu", p + (8, 0, 16)[i]), Y3[:, i, 1:1 + T], ALU.mult, ALU.add
                    ).then_inc((kv if i == 0 else fv).sem, 1)

            def log_decay(l, p):
                dve.wait_ge(fa.sem, fa.after(l, p, "lw"))
                dve.tensor_tensor_scan(CC[:, 0:TP], scan_keep, LW[:, 0:TP], 0.0, ALU.mult, ALU.add
                                       ).then_inc(fv.sem, 1)

            def rate(l, p):
                dve.wait_ge(fa.sem, fa.after(l, p, "a"))
                dve.tensor_scalar(T1, A, P("k_a", p), P("k_a", p), ALU.mult, ALU.subtract).then_inc(fv.sem, 1)

            def key_scale(l, p):
                dve.wait_ge(fa.sem, fa.after(l, p, "rtk"))
                dve.tensor_scalar(KQ, KQ, 1e-12, None, ALU.max).then_inc(fv.sem, 1)
                dve.wait_ge(fv.sem, fv.after(l, p, "inv0"))
                dve.reciprocal(KQ, KQ).then_inc(fv.sem, 1)
                dve.wait_ge(fv.sem, fv.after(l, p, "inv"))
                stt(KK, Kx, P("k_k", p), KQ, ALU.mult, ALU.mult).then_inc(fv.sem, 1)

            def keys(l, p):
                dve.wait_ge(fv.sem, fv.after(l, p, "t1"))
                stt(KP, T1, 1.0, Kx, ALU.add, ALU.mult).then_inc(fv.sem, 1)
                dve.wait_ge(fv.sem, fv.after(l, p, "kk"))
                stt(A, KK, -1.0, A, ALU.mult, ALU.mult).then_inc(fv.sem, 1)

            def bonus_rows(l, p):
                stt(T1, R, P("r_k", p), KP, ALU.mult, ALU.mult).then_inc(fv.sem, 1)

            def against(l, p):
                dve.wait_ge(fa.sem, fa.after(l, p, "ip"))
                dve.wait_ge(fv.sem, fv.after(l, p, "b"))
                tt(slots(BK)[:, :, 0:4:3, :], tokens(A), tokens(CC), ALU.mult).then_inc(fv.sem, 1)
                tt(slots(BK)[:, :, 1:3, :], tokens(KP), tokens(CC), ALU.mult).then_inc(fv.sem, 1)

            def along(l, p):
                dve.wait_ge(bp.sem, bp.after(l, p - 1, f"y_{NC - 1}"))
                dve.wait_ge(bv.sem, bv.after(l, p - 1, f"sh_{NC - 1}"))
                dve.tensor_copy(PEND.unsqueeze(2), pc[:, :, C - 1:C]).then_inc(fv.sem, 1)
                tt(AR[:, :, 1:C], kc[:, :, 1:C], pc[:, :, 0:C - 1], ALU.mult).then_inc(fv.sem, 1)
                dve.tensor_copy(AR[:, :, 0:1], kc[:, :, 0:1]).then_inc(fv.sem, 1)
                tt(AR[:, :, C:], rc, pc, ALU.mult).then_inc(fv.sem, 1)

            def hat(l, p):
                dve.wait_ge(fv.sem, fv.after(l, p, "bk_k"))
                tt(BKH, BK, pc[:, :, C - 1:C].broadcast_to([128, NC, 128]), ALU.mult).then_inc(fv.sem, 1)

            def bonus(l, p):
                dve.wait_ge(fp.sem, fp.after(l, p, "bon"))
                dve.wait_ge(hv.sem, hv.after(l, p - 1, "z"))
                dve.wait_ge(bon_g.sem, bon_g.after(l, p - 1, "s"))
                tt(two(BON), bank2(0, T // 2), two(V), ALU.mult).then_inc(fv.sem, 1)
                tt(GG, GT, GA, ALU.mult).then_inc(fv.sem, 1)

            def masked(l, p):
                for h in range(2):
                    dve.wait_ge(fp.sem, fp.after(l, p, f"g{h}"))
                    g = PS[:, 6 - 6 * h:8 - 6 * h, :].rearrange("p a (c t) -> p (a c) t", t=128)
                    tt(GM[:, h], g, mask8.unsqueeze(1).broadcast_to([128, NC, 128]), ALU.mult).then_inc(fv.sem, 1)

            def flat(x):
                return x.rearrange("p a b c -> p (a b c)")

            def level(l, p, i):
                if i == 0:
                    for q in range(2):
                        r = slice(64 * q, 64 * q + 64)
                        dve.wait_ge(fv.sem, fv.after(l, p, "g1"))
                        tt(U[r], GM[r, :, q::2, 0:C],
                           lev[r, 0, :].unsqueeze(1).unsqueeze(1).broadcast_to([64, 2, NC // 2, C]), ALU.mult
                           ).then_inc(bv.sem, 1)
                    dve.wait_ge(bv.sem, bv.after(l, p, "m0"))
                    tt(U, U, i64.unsqueeze(1).unsqueeze(1).broadcast_to([128, 2, NC // 2, C]), ALU.add
                       ).then_inc(bv.sem, 1)
                    return
                dve.wait_ge(bp.sem, bp.after(l, p, f"t{i}" if i < LEVELS - 1 else f"z{i}"))
                tt(flat(U), PS[:, 6, :], flat(U), ALU.add).then_inc(bv.sem, 1)
                if i < LEVELS - 1:
                    if i == 1:
                        dve.wait_ge(ba.sem, ba.after(l, p, "x0"))
                    tt(flat(XI), PS[:, 7, :], flat(XI), ALU.add).then_inc(bv.sem, 1)

            def chunk(l, p, c):
                r = slice(64 * (c % 2), 64 * (c % 2) + 64)
                dve.wait_ge(bp.sem, bp.after(l, p, f"sa_{c}"))
                if c == 0:
                    dve.wait_ge(fa.sem, fa.after(l, p, "tz"))
                dve.tensor_copy(W[r, c, :], PS[r, 5, 0:128]).then_inc(bv.sem, 1)
                dve.wait_ge(bp.sem, bp.after(l, p, f"s_{c}"))
                for h in range(2):
                    hr = slice(64 * h, 64 * h + 64)
                    now = S0[hr, h * N:h * N + N]
                    new = now if c < NC - 1 else STO[hr, bass.ds(p, 1), :].rearrange("p a b -> p (a b)")
                    if c == 0:
                        dve.tensor_copy(new, PS[hr, 6, 0:N]).then_inc(bv.sem, 1)
                    else:
                        stt(new, now, PEND[hr, c:c + 1], PS[hr, 6, 0:N], ALU.mult, ALU.add).then_inc(bv.sem, 1)

            def head_centre(l, p):
                dve.wait_ge(hp.sem, hp.after(l, p, "mean"))
                stt(YO, PS[:, 2, :], -1.0 / N, YO, ALU.mult, ALU.add).then_inc(hv.sem, 1)

            def head_scale(l, p):
                dve.wait_ge(ha.sem, ha.after(l, p, "rt"))
                dve.reciprocal(SQ, SQ).then_inc(hv.sem, 1)
                dve.wait_ge(hv.sem, hv.after(l, p, "ri"))
                tt(YO, YO, SQ, ALU.mult).then_inc(hv.sem, 1)

            def head_out(l, p):
                dve.wait_ge(hv.sem, hv.after(l, p, "gn"))
                dve.tensor_scalar(YO, YO, P("ln_x_g", p), P("ln_x_b", p), ALU.mult, ALU.add).then_inc(hv.sem, 1)
                dve.wait_ge(hv.sem, hv.after(l, p, "gnb"))
                tt(YO, YO, BON[:, 0:TP], ALU.add).then_inc(hv.sem, 1)
                dve.wait_ge(hv.sem, hv.after(l, p, "ob"))
                tt(Z[:, bass.ds(p, 1), 0:TP].rearrange("p a t -> p (a t)"), YO, GG[:, 0:TP], ALU.mult
                   ).then_inc(hv.sem, 1)

            def first_pair(l):
                mix(l, 0, 0)
                key_scale(l, 0)
                mix(l, 0, 1)
                log_decay(l, 0)
                mix(l, 0, 2)
                rate(l, 0)
                keys(l, 0)
                against(l, 0)
                along(l, 0)
                hat(l, 0)
                bonus_rows(l, 0)
                masked(l, 0)

            def step_of_pairs(l, p, first=False):
                n = p + 1
                for i in range(LEVELS):
                    level(l, p, i)
                    if i == 0:
                        tap(l, 4 * p + 1)
                        tap(l, 4 * p + 2)
                    if i == 1:
                        if not first:
                            head_centre(l, p - 1)
                        tap(l, 4 * p + 3)
                    if i == 2:
                        if not first:
                            head_scale(l, p - 1)
                        tap(l, 4 * p + 4, (0, 1))
                    if i == 3:
                        mix(l, n, 0)
                        if not first:
                            head_out(l, p - 1)
                        bonus(l, p)
                    if i == 4:
                        key_scale(l, n)
                for c in range(NC):
                    chunk(l, p, c)
                    if c == 0:
                        tap(l, 4 * p + 4, (2, 3))
                    if c == 2:
                        mix(l, n, 1)
                    if c == 3:
                        log_decay(l, n)
                    if c == 4:
                        mix(l, n, 2)
                    if c == 5:
                        rate(l, n)
                        keys(l, n)
                    if c == 6:
                        against(l, n)
                along(l, n)
                hat(l, n)
                bonus_rows(l, n)
                masked(l, n)

            def last_pair(l):
                p = PAIRS - 1
                for i in range(LEVELS):
                    level(l, p, i)
                    if i == 0:
                        tap(l, CW - 2)
                    if i == 1:
                        head_centre(l, p - 1)
                        tap(l, CW - 1)
                    if i == 2:
                        head_scale(l, p - 1)
                    if i == 3:
                        head_out(l, p - 1)
                        bonus(l, p)
                conv_centre(l)
                for c in range(NC):
                    chunk(l, p, c)
                    if c == 3:
                        conv_scale(l)
                head_centre(l, p)
                head_scale(l, p)
                head_out(l, p)

            def over_values(i, t):
                return QT[:, i, bass.ds(t, 1), :].broadcast_to([128, N, N])

            def over_keys(v):
                return v.unsqueeze(2).broadcast_to([128, N, N])

            def scan_step(l, t):
                dve.wait_ge(sp_v.sem, sp_v.after(l, t - 1, "r"))
                tt(M1, SS, over_values(3, t), ALU.mult).then_inc(sp_v.sem, 1)
                dve.wait_ge(sp_v.sem, sp_v.after(l, t, "m"))
                dve.tensor_reduce(SA, M1, AX.X, ALU.add).then_inc(sp_v.sem, 1)
                dve.wait_ge(sp_v.sem, sp_v.after(l, t, "sa"))
                tt(M1, over_keys(SA), over_values(4, t), ALU.mult).then_inc(sp_v.sem, 1)
                dve.wait_ge(sp_v.sem, sp_v.after(l, t, "u"))
                dve.wait_ge(sp_g.sem, sp_g.after(l, t, "sw"))
                tt(SS, SS, M1, ALU.add).then_inc(sp_v.sem, 1)
                dve.wait_ge(sp_v.sem, sp_v.after(l, t, "o"))
                dve.wait_ge(sp_g.sem, sp_g.after(l, t, "vk"))
                tt(SS, SS, M2, ALU.add).then_inc(sp_v.sem, 1)
                dve.wait_ge(sp_v.sem, sp_v.after(l, t, "v"))
                tt(M1, SS, over_values(5, t), ALU.mult).then_inc(sp_v.sem, 1)
                dve.wait_ge(sp_v.sem, sp_v.after(l, t, "y"))
                dve.tensor_reduce(SY[:, bass.ds(t, 1), :].rearrange("p a b -> p (a b)"), M1, AX.X, ALU.add
                                  ).then_inc(sp_v.sem, 1)

            def late(l, m, b):
                dve.wait_ge(gemm.sem, tile_after(l, Q_LATE + m, 1))
                dve.wait_ge(late_a.sem, late_a.after(l, m, "gb"))
                dve.wait_ge(late_g.sem, late_g.after(l, m - 2, "zs"))
                tt(two(OB[b]), bank2(2 * b + 1, T // 2), two(GB[b]), ALU.mult).then_inc(late_v.sem, 1)

            def sample_out(l):
                def across(name):
                    return par_sb[:, COL[name]:COL[name] + PAIRS].unsqueeze(2).broadcast_to([128, PAIRS, TS])

                def step(name, out, a, b, op):
                    if name:
                        dve.wait_ge(spo_v.sem, spo_v.after(l, 0, name))
                    tt(out, a, b, op).then_inc(spo_v.sem, 1)
                mean = PS[:, 2, 0:PAIRS * TS].rearrange("p (a t) -> p a t", a=PAIRS)
                dve.wait_ge(sp_p.sem, sp_p.after(l, 0, "mean"))
                stt(YF, mean, -1.0 / N, YF, ALU.mult, ALU.add).then_inc(spo_v.sem, 1)
                dve.wait_ge(sp_a.sem, sp_a.after(l, 0, "rt"))
                dve.reciprocal(YR, YR).then_inc(spo_v.sem, 1)
                step("ri", YF, YF, YR, ALU.mult)
                step("gn", YF, YF, across("ln_x_g"), ALU.mult)
                step("g", YF, YF, across("ln_x_b"), ALU.add)
                step("b", YF, YF, SX[:, :, 0, :], ALU.add)
                step("ob", YF, YF, SX[:, :, 1, :], ALU.mult)
                step("og", YF, YF, SX[:, :, 2, :], ALU.mult)
                dve.wait_ge(late_g.sem, late_g.after(l, KT - 1, "zs"))
                step("oa", Z[:, :, TP:T], Z[:, :, TP:T], YF, ALU.add)

            def mix_out(l):
                alone(dve)
                with dve.Fori(0, KT // 4) as j:
                    for b in range(4):
                        m = 4 * j + b
                        dve.wait_ge(gemm.sem, tile_after(l, Q_OUT + 2 * j + b // 2, b % 2))
                        x = X2[:, bass.ds(2 * m, 2), :]
                        tt(x, bank2(b, T // 2), x, ALU.add).then_inc(xdone.sem, 1)

            with dve.Fori(0, L) as l:
                dve.wait_ge(par_load, l * 16 + 16)
                norm(l, 0, lambda k: P("ffn1_norm", k))
                ffn(l, 0, Q_FFN1)
                dve.wait_ge(xdone.sem, xdone.after(l, 0, f"m{KT - 1}"))
                dve.tensor_copy(H[:, :, T:TH], shf_sb[:, bass.ds(l, 1), :, :].rearrange("p a k b -> p (a k) b")
                                ).then_inc(prev_v.sem, 1)
                norm(l, 1, lambda k: P("mix_norm", k))
                dve.wait_ge(norm_v.sem, norm_v.after(l, 1, f"h{KT - 1}"))
                dve.tensor_copy(sho[:, bass.ds(l, 1), :, 0:1].rearrange("p a k b -> p (a k) b"),
                                H[:, :, TP - 1:TP]).then_inc(prev_v.sem, 1)
                dve.tensor_copy(sho[:, bass.ds(l, 1), :, 1:].rearrange("p a k b -> p (a k) b"),
                                H[:, :, TP + NT - 1:T:NT]).then_inc(prev_v.sem, 1)
                lora(l)
                glu(l)
                first_tap(l)
                first_pair(l)
                step_of_pairs(l, 0, first=True)
                alone(dve)
                with dve.Fori(1, PAIRS - 1) as p:
                    step_of_pairs(l, p)
                last_pair(l)
                dve.wait_ge(hv.sem, hv.after(l, PAIRS - 1, "z"))
                dve.wait_ge(bon_g.sem, bon_g.after(l, PAIRS - 1, "s"))
                dve.wait_ge(q_got, l * NB * 16 + NB * 16)
                dve.wait_ge(s_load, l * 16 + 16)
                alone(dve)
                with dve.Fori(0, NT) as t:
                    scan_step(l, t)
                    for b in range(2):
                        late(l, 2 * t + b, b)
                sample_out(l)
                mix_out(l)
                norm(l, 2, lambda k: P("ffn2_norm", k))
                ffn(l, 1, Q_FFN2)
            norm(L, 0, lambda k: fn_sb[:, k:k + 1])


def constants():
    k = np.zeros((128, K_ALL), np.float32)
    row, col = np.arange(128)[:, None], np.arange(128)[None, :]
    s, t = np.arange(128)[:, None] % 64, np.arange(64)[None, :]
    k[:, K_ID:K_ID + 128] = row == col
    k[:, K_ONE:K_ONE + 128] = 1
    k[:, K_BLK:K_BLK + 128] = row // 64 == col // 64
    k[:, K_MASK:K_MASK + 64] = s < t
    k[:, K_MASK + 64:K_MASK + 128] = s <= t
    for i in range(LEVELS):
        b = 1 << i
        k[:, K_LEV + 64 * i:K_LEV + 64 * i + 64] = (s // (2 * b) == t // (2 * b)) & (s % (2 * b) < b) & (t % (2 * b) >= b)
    k[:, K_I64:K_I64 + 64] = s == t
    k[:, K_SCAN:K_SCAN + TP] = np.arange(TP)[None, :] % C != 0
    k[:, K_EPS], k[:, K_EPS + 1], k[:, K_EPS + 2] = NORM_EPS, GN_EPS, LN_EPS
    return k


def kernel(**inputs):
    import concourse.bacc as bacc
    from concourse.bass_utils import run_bass_kernel_spmd

    a = {k: np.asarray(v) for k, v in inputs.items()}
    x = np.concatenate([a["x_prompt"].reshape(TP, D), a["x_sample"].reshape(TS, D)])

    def tiles(w, cols):
        part = w[:, cols * 128:cols * 128 + 128]
        return part.reshape(-1, 128, 128).transpose(1, 0, 2).reshape(128, -1)

    def both(u, v):
        return np.concatenate([u, v], axis=1)

    wr, wpa, wpb, wl, wd = [], [], [], [], []
    for l in range(L):
        win = a["w_in"][l]

        def ffn(f):
            wr.extend(both(tiles(a[f + "_w_gate"][l], t), tiles(a[f + "_w_up"][l], t)) for t in range(FT))
            wd.extend(tiles(a[f + "_w_down"][l], m) for m in range(KT))
        ffn("ffn1")
        wr.append(both(tiles(win, 24), tiles(win, 25)))
        wr.extend(both(tiles(win, 26 + c), tiles(win, 30 + c)) for c in range(CT))
        for p in range(PAIRS):
            cols = slice(p * 128, p * 128 + 128)
            wpa.append(both(tiles(win, 8 + p), tiles(win, p)))
            low = np.concatenate([a["w_decay_up"][l][:, cols], a["w_iclr_up"][l][:, cols]])
            wpb.append(np.concatenate([tiles(win, 16 + p), tiles(win, 34 + p), low, a["w_gate_up"][l][:, cols]], axis=1))
        wl.extend(both(tiles(win, 42 + m), tiles(a["w_conv_out"][l], m)) for m in range(KT))
        wr.extend(both(tiles(a["w_out"][l], 2 * i), tiles(a["w_out"][l], 2 * i + 1)) for i in range(KT // 2))
        ffn("ffn2")
    par = []
    for name, n in PARAMS:
        if name == "conv_w":
            par.append(a[name].reshape(L, CW, CT, 128).transpose(0, 3, 2, 1).reshape(L, 128, n))
        else:
            par.append(a[name].reshape(L, n, 128).transpose(0, 2, 1))
    hist = a["state_conv"].reshape(L, NB, HIST, CT, 128).transpose(0, 4, 3, 1, 2)
    hist = np.concatenate([hist, np.zeros((L, 128, CT, NB, NT), np.float32)], axis=-1)
    arrays = {
        "xt": x.reshape(T, KT, 128).transpose(2, 1, 0),
        "par": np.concatenate(par, axis=2),
        "fnorm": a["final_norm"].reshape(KT, 128).T,
        "shf": a["state_shift"].reshape(L, NB, KT, 128).transpose(3, 0, 2, 1),
        "cs": hist.reshape(L, 128, -1),
        "s_in": a["state_wkv"].reshape(L, NB * NH, N * N),
        "wr": np.stack(wr), "wpa": np.stack(wpa), "wpb": np.stack(wpb), "wl": np.stack(wl), "wd": np.stack(wd),
        "consts": constants(),
    }
    arrays = {k: np.ascontiguousarray(v) for k, v in arrays.items()}
    outs = {"y": (128, KT, T), "wkvp": (L, 128, PAIRS * C), "shift": (128, L, KT, 1 + NB),
            "convp": (L, 128, CT, HIST), "wkvs": (L, 128, N * N), "convs": (L, 128, CT * NB * (HIST + NT))}
    nc = bacc.Bacc("TRN2", target_bir_lowering=False, num_devices=1)
    args = [nc.dram_tensor(k, v.shape, F32, kind="ExternalInput").ap() for k, v in arrays.items()]
    args += [nc.dram_tensor("out_" + k, s, F32, kind="ExternalOutput").ap() for k, s in outs.items()]
    build(nc, *args)
    r = run_bass_kernel_spmd(nc, [arrays], core_ids=[0]).results[0]
    got = {k: np.asarray(r["out_" + k]) for k in outs}
    y = got["y"].transpose(2, 1, 0).reshape(T, D)
    shift = got["shift"].transpose(1, 3, 2, 0).reshape(L, 1 + NB, D)
    wkvp = got["wkvp"].reshape(L, 2, N, PAIRS, C).transpose(0, 3, 1, 4, 2).reshape(L, 1, NH, N, N)
    convs = got["convs"].reshape(L, 128, CT, NB, HIST + NT)[..., NT:].transpose(0, 3, 4, 2, 1)
    return (y[:TP].reshape(1, TP, D), y[TP:].reshape(NB, NT, D), wkvp, shift[:, :1],
            got["convp"].transpose(0, 3, 2, 1).reshape(L, 1, HIST, DC),
            got["wkvs"].reshape(L, NB, NH, N, N), shift[:, 1:], convs.reshape(L, NB, HIST, DC))
```
